# Optimizing a Trainium2 kernel written in Bass

```python
import math
import jax, jax.numpy as jnp
from jax import lax
import numpy as np

D_MODEL = 1024
BATCH = 1
SEQ = 512
DEPTH = 1

N_HEADS = 16
HEAD_DIM = 64
N_KV_GROUPS = 4
HEADS_PER_GROUP = N_HEADS // N_KV_GROUPS
CMP_BLOCK = 32
CMP_STRIDE = 16
CMP_HIDDEN = 256
SEL_BLOCK = 64
N_SELECT = 16
WINDOW = 512
NSA_Q_BLOCK = 64
FORCE = 1e4
CONV_DIM = D_MODEL
CONV_WIDTH = 3
N_MEM = 256
MEM_HEADS = 4
MEM_HEAD_DIM = D_MODEL // MEM_HEADS
REL_BUCKETS = 32
REL_MAX_DIST = 128
D_FF = 2816
EPS = 1e-6
NEG = -1e30

NSA_WIDTH = N_HEADS * HEAD_DIM
KV_WIDTH = N_KV_GROUPS * HEAD_DIM
MEM_WIDTH = MEM_HEADS * MEM_HEAD_DIM
IN_SPLITS = (NSA_WIDTH, 6 * KV_WIDTH, 3 * N_HEADS, 3 * CONV_DIM, MEM_WIDTH, 3 * D_MODEL)
IN_WIDTH = NSA_WIDTH + 6 * KV_WIDTH + 3 * N_HEADS + 3 * CONV_DIM + MEM_WIDTH + 3 * D_MODEL


def rmsnorm(x, g):
    xf = x.astype(jnp.float32)
    y = xf * lax.rsqrt(jnp.mean(xf * xf, axis=-1, keepdims=True) + EPS)
    return (y * g.astype(jnp.float32)).astype(x.dtype)

def swiglu_ffn(h, w_in, w_out):
    a, b = jnp.split(h @ w_in, 2, axis=-1)
    return (jax.nn.silu(a) * b) @ w_out

def masked_softmax(s, valid):
    return jax.nn.softmax(jnp.where(valid, s.astype(jnp.float32), NEG), axis=-1)

def rel_bucket(dist):
    n = jnp.maximum(dist, 0)
    max_exact = REL_BUCKETS // 2
    nf = jnp.maximum(n, 1).astype(jnp.float32)
    large = max_exact + (jnp.log(nf / max_exact) / math.log(REL_MAX_DIST / max_exact)
                         * (REL_BUCKETS - max_exact)).astype(jnp.int32)
    large = jnp.minimum(large, REL_BUCKETS - 1)
    return jnp.where(n < max_exact, n, large)

def compress(kv, pe, w1, w2):
    b, s, g, d = kv.shape
    ratio = CMP_BLOCK // CMP_STRIDE
    n_chunks = s // CMP_STRIDE
    chunks = kv.reshape(b, n_chunks, CMP_STRIDE, g, d)
    blocks = jnp.concatenate([chunks[:, r:n_chunks - ratio + 1 + r] for r in range(ratio)], axis=2)
    blocks = blocks + pe[None, None, :, None, :]
    n_cmp = blocks.shape[1]
    flat = blocks.transpose(0, 1, 3, 2, 4).reshape(b, n_cmp, g, CMP_BLOCK * d)
    return jax.nn.silu(flat @ w1) @ w2

def cmp_to_sel_matrix(n_cmp, n_sel):
    cs = jnp.arange(n_cmp)[:, None] * CMP_STRIDE
    ss = jnp.arange(n_sel)[None, :] * SEL_BLOCK
    ov = jnp.maximum(jnp.minimum(cs + CMP_BLOCK, ss + SEL_BLOCK) - jnp.maximum(cs, ss), 0)
    return ov.astype(jnp.float32) / CMP_BLOCK

def nsa_attention(q, k_cmp, v_cmp, k_slc, v_slc, k_win, v_win, gates, rel_bias):
    b, s, h, d = q.shape
    g, r = N_KV_GROUPS, HEADS_PER_GROUP
    n_cmp = k_cmp.shape[1]
    n_sel = s // SEL_BLOCK
    top = min(N_SELECT, n_sel)
    scale = d ** -0.5
    qg = q.reshape(b, s, g, r, d)
    gg = gates.reshape(b, s, g, r, 3)
    bias_grk = rel_bias.reshape(REL_BUCKETS, g, r).transpose(1, 0, 2)
    sel_map = cmp_to_sel_matrix(n_cmp, n_sel)
    cmp_end = jnp.arange(n_cmp) * CMP_STRIDE + CMP_BLOCK - 1
    ks_blocks = k_slc.reshape(b, n_sel, SEL_BLOCK, g, d).transpose(0, 3, 1, 2, 4)
    vs_blocks = v_slc.reshape(b, n_sel, SEL_BLOCK, g, d).transpose(0, 3, 1, 2, 4)
    pad = ((0, 0), (WINDOW, 0), (0, 0), (0, 0))
    kw_pad = jnp.pad(k_win, pad)
    vw_pad = jnp.pad(v_win, pad)
    bi = jnp.arange(b)[:, None, None, None]
    gi = jnp.arange(g)[None, :, None, None]

    def dense_bias(dist):
        qn, kn = dist.shape
        return rel_bias[rel_bucket(dist)].reshape(qn, kn, g, r).transpose(2, 3, 0, 1)

    def block(i):
        s0 = i * NSA_Q_BLOCK
        t = s0 + jnp.arange(NSA_Q_BLOCK)
        qb = lax.dynamic_slice_in_dim(qg, s0, NSA_Q_BLOCK, axis=1)
        gb = lax.dynamic_slice_in_dim(gg, s0, NSA_Q_BLOCK, axis=1)
        valid_c = cmp_end[None, :] <= t[:, None]
        s_c = jnp.einsum('bqgrd,bcgd->bgrqc', qb, k_cmp) * scale + dense_bias(t[:, None] - cmp_end[None, :])
        p_c = masked_softmax(s_c, valid_c) * jnp.any(valid_c, axis=-1)[:, None].astype(jnp.float32)
        o_c = jnp.einsum('bgrqc,bcgd->bqgrd', p_c.astype(v_cmp.dtype), v_cmp)
        imp = jnp.einsum('bgrqc,cn->bgqn', p_c, sel_map)
        blk = jnp.arange(n_sel)[None, :]
        cur = (t // SEL_BLOCK)[:, None]
        valid_b = blk <= cur
        forced = (blk == 0) | (blk == cur) | (blk == cur - 1)
        score = jnp.where(valid_b, imp + jnp.where(forced, FORCE, 0.0), -FORCE)
        _, idx = lax.top_k(score, top)
        ks = ks_blocks[bi, gi, idx].reshape(b, g, NSA_Q_BLOCK, top * SEL_BLOCK, d)
        vs = vs_blocks[bi, gi, idx].reshape(b, g, NSA_Q_BLOCK, top * SEL_BLOCK, d)
        pos = (idx[..., None] * SEL_BLOCK + jnp.arange(SEL_BLOCK)).reshape(b, g, NSA_Q_BLOCK, top * SEL_BLOCK)
        dist_s = t[None, None, :, None] - pos
        bias_s = bias_grk[gi, rel_bucket(dist_s)].transpose(0, 1, 4, 2, 3)
        s_s = jnp.einsum('bqgrd,bgqtd->bgrqt', qb, ks) * scale + bias_s
        p_s = masked_softmax(s_s, (dist_s >= 0)[:, :, None])
        o_s = jnp.einsum('bgrqt,bgqtd->bqgrd', p_s.astype(vs.dtype), vs)
        kw = lax.dynamic_slice_in_dim(kw_pad, s0, NSA_Q_BLOCK + WINDOW, axis=1)
        vw = lax.dynamic_slice_in_dim(vw_pad, s0, NSA_Q_BLOCK + WINDOW, axis=1)
        kp = s0 - WINDOW + jnp.arange(NSA_Q_BLOCK + WINDOW)
        dist_w = t[:, None] - kp[None, :]
        valid_w = (kp[None, :] >= 0) & (dist_w >= 0) & (dist_w < WINDOW)
        s_w = jnp.einsum('bqgrd,bkgd->bgrqk', qb, kw) * scale + dense_bias(dist_w)
        p_w = masked_softmax(s_w, valid_w)
        o_w = jnp.einsum('bgrqk,bkgd->bqgrd', p_w.astype(vw.dtype), vw)
        return gb[..., 0:1] * o_c + gb[..., 1:2] * o_s + gb[..., 2:3] * o_w

    out = lax.map(block, jnp.arange(s // NSA_Q_BLOCK))
    return out.transpose(1, 0, 2, 3, 4, 5).reshape(b, s, h * d)

def short_gated_conv(conv_in, conv_w, conv_b):
    gate_b, gate_c, x_in = jnp.split(conv_in, 3, axis=-1)
    u = gate_c * x_in
    y = lax.conv_general_dilated(u, conv_w[:, None, :], window_strides=(1,),
                                 padding=((CONV_WIDTH - 1, 0),),
                                 dimension_numbers=('NWC', 'WIO', 'NWC'),
                                 feature_group_count=u.shape[-1])
    return gate_b * (y + conv_b)

def memory_attention(q_mem, mem, mem_norm_g, w_mem_kv, q_g, k_g):
    b, s, _ = q_mem.shape
    m = mem.shape[1]
    km, vm = jnp.split(rmsnorm(mem, mem_norm_g) @ w_mem_kv, 2, axis=-1)
    km = rmsnorm(km.reshape(b, m, MEM_HEADS, MEM_HEAD_DIM), k_g)
    vm = vm.reshape(b, m, MEM_HEADS, MEM_HEAD_DIM)
    qm = rmsnorm(q_mem.reshape(b, s, MEM_HEADS, MEM_HEAD_DIM), q_g)
    sm = jnp.einsum('bshd,bmhd->bhsm', qm, km) * MEM_HEAD_DIM ** -0.5
    pm = jax.nn.softmax(sm.astype(jnp.float32), axis=-1).astype(vm.dtype)
    return jnp.einsum('bhsm,bmhd->bshd', pm, vm).reshape(b, s, MEM_WIDTH)

def hybrid_layer(x, mem, ffn1_norm_g, ffn1_w_in, ffn1_w_out, mix_norm_g, w_in, q_norm_g, k_norm_g,
                 cmp_pe_k, cmp_w1_k, cmp_w2_k, cmp_pe_v, cmp_w1_v, cmp_w2_v, conv_w, conv_b,
                 mem_norm_g, w_mem_kv, mem_q_norm_g, mem_k_norm_g, w_out,
                 ffn2_norm_g, ffn2_w_in, ffn2_w_out, rel_bias):
    b, s, _ = x.shape
    x = x + 0.5 * swiglu_ffn(rmsnorm(x, ffn1_norm_g), ffn1_w_in, ffn1_w_out)
    h = rmsnorm(x, mix_norm_g)
    split_points = np.cumsum(IN_SPLITS)[:-1].tolist()
    q, kv, nsa_g, conv_in, q_mem, merge_g = jnp.split(h @ w_in, split_points, axis=-1)
    q = rmsnorm(q.reshape(b, s, N_HEADS, HEAD_DIM), q_norm_g)
    kc, vc, ks, vs, kw, vw = [t.reshape(b, s, N_KV_GROUPS, HEAD_DIM) for t in jnp.split(kv, 6, axis=-1)]
    k_cmp = rmsnorm(compress(kc, cmp_pe_k, cmp_w1_k, cmp_w2_k), k_norm_g)
    v_cmp = compress(vc, cmp_pe_v, cmp_w1_v, cmp_w2_v)
    gates = jax.nn.sigmoid(nsa_g.astype(jnp.float32)).astype(x.dtype).reshape(b, s, N_HEADS, 3)
    o_nsa = nsa_attention(q, k_cmp, v_cmp, rmsnorm(ks, k_norm_g), vs, rmsnorm(kw, k_norm_g), vw,
                          gates, rel_bias)
    o_conv = short_gated_conv(conv_in, conv_w, conv_b)
    o_mem = memory_attention(q_mem, mem, mem_norm_g, w_mem_kv, mem_q_norm_g, mem_k_norm_g)
    g_nsa, g_conv, g_mem = jnp.split(jax.nn.sigmoid(merge_g.astype(jnp.float32)).astype(x.dtype), 3, axis=-1)
    x = x + (g_nsa * o_nsa + g_conv * o_conv + g_mem * o_mem) @ w_out
    x = x + 0.5 * swiglu_ffn(rmsnorm(x, ffn2_norm_g), ffn2_w_in, ffn2_w_out)
    return x

def first_inputs(seed: int = 0) -> dict:
    key = jax.random.key(seed)
    keys = iter(jax.random.split(key, 32))
    L = DEPTH

    def nrm(shape, scale):
        return jax.random.normal(next(keys), shape, jnp.float32) * scale

    def w(shape, fan_in):
        return nrm(shape, fan_in ** -0.5)

    def gain(shape):
        return 1.0 + nrm(shape, 0.05)

    return {
        "x": nrm((BATCH, SEQ, D_MODEL), 1.0),
        "mem": nrm((BATCH, N_MEM, D_MODEL), 1.0),
        "ffn1_norm_g": gain((L, D_MODEL)),
        "ffn1_w_in": w((L, D_MODEL, 2 * D_FF), D_MODEL),
        "ffn1_w_out": w((L, D_FF, D_MODEL), D_FF),
        "mix_norm_g": gain((L, D_MODEL)),
        "w_in": w((L, D_MODEL, IN_WIDTH), D_MODEL),
        "q_norm_g": gain((L, HEAD_DIM)),
        "k_norm_g": gain((L, HEAD_DIM)),
        "cmp_pe_k": nrm((L, CMP_BLOCK, HEAD_DIM), 0.1),
        "cmp_w1_k": w((L, CMP_BLOCK * HEAD_DIM, CMP_HIDDEN), CMP_BLOCK * HEAD_DIM),
        "cmp_w2_k": w((L, CMP_HIDDEN, HEAD_DIM), CMP_HIDDEN),
        "cmp_pe_v": nrm((L, CMP_BLOCK, HEAD_DIM), 0.1),
        "cmp_w1_v": w((L, CMP_BLOCK * HEAD_DIM, CMP_HIDDEN), CMP_BLOCK * HEAD_DIM),
        "cmp_w2_v": w((L, CMP_HIDDEN, HEAD_DIM), CMP_HIDDEN),
        "conv_w": w((L, CONV_WIDTH, CONV_DIM), CONV_WIDTH),
        "conv_b": nrm((L, CONV_DIM), 0.02),
        "mem_norm_g": gain((L, D_MODEL)),
        "w_mem_kv": w((L, D_MODEL, 2 * MEM_WIDTH), D_MODEL),
        "mem_q_norm_g": gain((L, MEM_HEAD_DIM)),
        "mem_k_norm_g": gain((L, MEM_HEAD_DIM)),
        "w_out": w((L, D_MODEL, D_MODEL), D_MODEL),
        "ffn2_norm_g": gain((L, D_MODEL)),
        "ffn2_w_in": w((L, D_MODEL, 2 * D_FF), D_MODEL),
        "ffn2_w_out": w((L, D_FF, D_MODEL), D_FF),
        "rel_bias": nrm((REL_BUCKETS, N_HEADS), 0.5),
    }

def first_block(x, mem, ffn1_norm_g, ffn1_w_in, ffn1_w_out, mix_norm_g, w_in, q_norm_g, k_norm_g,
              cmp_pe_k, cmp_w1_k, cmp_w2_k, cmp_pe_v, cmp_w1_v, cmp_w2_v, conv_w, conv_b,
              mem_norm_g, w_mem_kv, mem_q_norm_g, mem_k_norm_g, w_out,
              ffn2_norm_g, ffn2_w_in, ffn2_w_out, rel_bias):
    for l in range(DEPTH):
        x = hybrid_layer(x, mem, ffn1_norm_g[l], ffn1_w_in[l], ffn1_w_out[l], mix_norm_g[l], w_in[l],
                         q_norm_g[l], k_norm_g[l], cmp_pe_k[l], cmp_w1_k[l], cmp_w2_k[l],
                         cmp_pe_v[l], cmp_w1_v[l], cmp_w2_v[l], conv_w[l], conv_b[l],
                         mem_norm_g[l], w_mem_kv[l], mem_q_norm_g[l], mem_k_norm_g[l], w_out[l],
                         ffn2_norm_g[l], ffn2_w_in[l], ffn2_w_out[l], rel_bias)
    return x


DEPTH_2 = 2

HEAD_DIM_2 = D_MODEL // N_HEADS
HD = N_HEADS * HEAD_DIM_2
D_FF_2 = ((8 * D_MODEL + 3 * 256 - 1) // (3 * 256)) * 256
PLE_DIM = 256
BLOCK_Q = 128
N_A = DEPTH_2 // 2
N_B = DEPTH_2 - N_A


def rms_norm(x, g):
    xf = x.astype(jnp.float32)
    y = xf * lax.rsqrt(jnp.mean(xf * xf, axis=-1, keepdims=True) + EPS)
    return (y * g.astype(jnp.float32)).astype(x.dtype)

def split_heads(t):
    b, s, _ = t.shape
    return t.reshape(b, s, N_HEADS, HEAD_DIM_2).transpose(0, 2, 1, 3)

def merge_heads(t):
    b, h, s, d = t.shape
    return t.transpose(0, 2, 1, 3).reshape(b, s, h * d)

def to_blocks(t):
    b, h, s = t.shape[:3]
    t = t.reshape((b, h, s // BLOCK_Q, BLOCK_Q) + t.shape[3:])
    return jnp.moveaxis(t, 2, 0)

def from_blocks(t):
    t = jnp.moveaxis(t, 0, 2)
    b, h, nb, bq, d = t.shape
    return t.reshape(b, h, nb * bq, d)

def stick_breaking_attention(q, k, v):
    s_len = q.shape[2]
    nb = s_len // BLOCK_Q
    kpos = jnp.arange(s_len)
    scale = HEAD_DIM_2 ** -0.5

    def block(args):
        qb, i = args
        tpos = i * BLOCK_Q + jnp.arange(BLOCK_Q)
        z = jnp.einsum('bhqd,bhkd->bhqk', qb, k).astype(jnp.float32) * scale
        strict = kpos[None, :] < tpos[:, None]
        log_one_minus = jnp.where(strict, -jax.nn.softplus(z), 0.0)
        later = lax.cumsum(log_one_minus, axis=3, reverse=True) - log_one_minus
        w = jnp.where(strict, jnp.exp(jax.nn.log_sigmoid(z) + later), 0.0)
        return jnp.einsum('bhqk,bhkd->bhqd', w.astype(v.dtype), v)

    out = lax.map(block, (to_blocks(q), jnp.arange(nb)))
    return from_blocks(out)

def forgetting_attention(q, k, v, f_cum):
    s_len = q.shape[2]
    nb = s_len // BLOCK_Q
    kpos = jnp.arange(s_len)
    scale = HEAD_DIM_2 ** -0.5

    def block(args):
        qb, fb, i = args
        tpos = i * BLOCK_Q + jnp.arange(BLOCK_Q)
        logits = (jnp.einsum('bhqd,bhkd->bhqk', qb, k).astype(jnp.float32) * scale
                  + fb[..., :, None] - f_cum[:, :, None, :])
        causal = kpos[None, :] <= tpos[:, None]
        logits = jnp.where(causal, logits, -jnp.inf)
        probs = jax.nn.softmax(logits, axis=-1)
        return jnp.einsum('bhqk,bhkd->bhqd', probs.astype(v.dtype), v)

    out = lax.map(block, (to_blocks(q), to_blocks(f_cum), jnp.arange(nb)))
    return from_blocks(out)

def swiglu(h, w_gu, w_d):
    g, u = jnp.split(h @ w_gu, 2, axis=-1)
    return (jax.nn.silu(g) * u) @ w_d

def second_inputs(seed: int = 0) -> dict:
    key = jax.random.key(seed)
    ks = jax.random.split(key, 20)
    f32 = jnp.float32

    def w(k, shape, fan_in, extra=1.0):
        return jax.random.normal(k, shape, f32) * (fan_in ** -0.5) * extra

    def gain(k, shape):
        return 1.0 + 0.05 * jax.random.normal(k, shape, f32)

    res_scale = (2.0 * DEPTH_2) ** -0.5
    return {
        'x': jax.random.normal(ks[0], (BATCH, SEQ, D_MODEL), f32),
        'p': jax.random.normal(ks[1], (DEPTH_2, BATCH, SEQ, PLE_DIM), f32),
        'attn_norm_g': gain(ks[2], (DEPTH_2, D_MODEL)),
        'sb_w_qkv': w(ks[3], (N_A, D_MODEL, 3 * HD), D_MODEL),
        'sb_w_o': w(ks[4], (N_A, HD, D_MODEL), HD, res_scale),
        'shared_norm_g': gain(ks[5], (D_MODEL,)),
        'shared_w_kvf': w(ks[6], (D_MODEL, 2 * HD + N_HEADS), D_MODEL),
        'shared_b_f': 0.1 * jax.random.normal(ks[7], (N_HEADS,), f32),
        'shared_k_norm_g': gain(ks[8], (HEAD_DIM_2,)),
        'fox_w_q': w(ks[9], (N_B, D_MODEL, HD), D_MODEL),
        'fox_q_norm_g': gain(ks[10], (N_B, HEAD_DIM_2)),
        'fox_w_o': w(ks[11], (N_B, HD, D_MODEL), HD, res_scale),
        'ffn_norm_g': gain(ks[12], (DEPTH_2, D_MODEL)),
        'ffn_w_gu': w(ks[13], (DEPTH_2, D_MODEL, 2 * D_FF_2), D_MODEL),
        'ffn_w_d': w(ks[14], (DEPTH_2, D_FF_2, D_MODEL), D_FF_2, res_scale),
        'ple_norm_g': gain(ks[15], (DEPTH_2, D_MODEL)),
        'ple_w_gate': w(ks[16], (DEPTH_2, D_MODEL, D_MODEL), D_MODEL),
        'ple_w_proj': w(ks[17], (DEPTH_2, PLE_DIM, D_MODEL), PLE_DIM, res_scale),
    }

def second_block(x, p, attn_norm_g, sb_w_qkv, sb_w_o, shared_norm_g, shared_w_kvf, shared_b_f,
              shared_k_norm_g, fox_w_q, fox_q_norm_g, fox_w_o, ffn_norm_g, ffn_w_gu, ffn_w_d,
              ple_norm_g, ple_w_gate, ple_w_proj):
    h = x
    k_sh = v_sh = f_cum = None
    for i in range(DEPTH_2):
        hn = rms_norm(h, attn_norm_g[i])
        if i < N_A:
            q, k, v = jnp.split(hn @ sb_w_qkv[i], 3, axis=-1)
            mix = stick_breaking_attention(split_heads(q), split_heads(k), split_heads(v))
            h = h + merge_heads(mix) @ sb_w_o[i]
        else:
            if i == N_A:
                hs = rms_norm(h, shared_norm_g)
                kvf = hs @ shared_w_kvf
                k_sh = rms_norm(split_heads(kvf[..., :HD]), shared_k_norm_g)
                v_sh = split_heads(kvf[..., HD:2 * HD])
                f_logit = kvf[..., 2 * HD:].astype(jnp.float32) + shared_b_f.astype(jnp.float32)
                f_cum = lax.cumsum(jax.nn.log_sigmoid(f_logit), axis=1).transpose(0, 2, 1)
            j = i - N_A
            q = rms_norm(split_heads(hn @ fox_w_q[j]), fox_q_norm_g[j])
            mix = forgetting_attention(q, k_sh, v_sh, f_cum)
            h = h + merge_heads(mix) @ fox_w_o[j]
        h = h + swiglu(rms_norm(h, ffn_norm_g[i]), ffn_w_gu[i], ffn_w_d[i])
        gate = jax.nn.sigmoid(rms_norm(h, ple_norm_g[i]) @ ple_w_gate[i])
        h = h + gate * (p[i] @ ple_w_proj[i])
    return h


def setup_inputs(seed=0):
    out = dict(first_inputs(seed))
    for name, value in second_inputs(seed + 1).items():
        if name != "x":
            out[name + "_2"] = value
    return out


def reference(
    x, mem, ffn1_norm_g, ffn1_w_in, ffn1_w_out, mix_norm_g, w_in, q_norm_g, k_norm_g, cmp_pe_k,
    cmp_w1_k, cmp_w2_k, cmp_pe_v, cmp_w1_v, cmp_w2_v, conv_w, conv_b, mem_norm_g, w_mem_kv,
    mem_q_norm_g, mem_k_norm_g, w_out, ffn2_norm_g, ffn2_w_in, ffn2_w_out, rel_bias, p_2,
    attn_norm_g_2, sb_w_qkv_2, sb_w_o_2, shared_norm_g_2, shared_w_kvf_2, shared_b_f_2,
    shared_k_norm_g_2, fox_w_q_2, fox_q_norm_g_2, fox_w_o_2, ffn_norm_g_2, ffn_w_gu_2,
    ffn_w_d_2, ple_norm_g_2, ple_w_gate_2, ple_w_proj_2,
):
    x = first_block(
        x, mem, ffn1_norm_g, ffn1_w_in, ffn1_w_out, mix_norm_g, w_in, q_norm_g, k_norm_g,
        cmp_pe_k, cmp_w1_k, cmp_w2_k, cmp_pe_v, cmp_w1_v, cmp_w2_v, conv_w, conv_b, mem_norm_g,
        w_mem_kv, mem_q_norm_g, mem_k_norm_g, w_out, ffn2_norm_g, ffn2_w_in, ffn2_w_out,
        rel_bias,
    )
    return second_block(
        x, p_2, attn_norm_g_2, sb_w_qkv_2, sb_w_o_2, shared_norm_g_2, shared_w_kvf_2,
        shared_b_f_2, shared_k_norm_g_2, fox_w_q_2, fox_q_norm_g_2, fox_w_o_2, ffn_norm_g_2,
        ffn_w_gu_2, ffn_w_d_2, ple_norm_g_2, ple_w_gate_2, ple_w_proj_2,
    )


_drawn_inputs = setup_inputs


def setup_inputs(seed=0):
    import zlib

    import numpy as np

    out = dict(_drawn_inputs(seed))
    spreads = {}
    factors = {'q_norm_g': 8.0,
     'k_norm_g': 8.0,
     'cmp_pe_k': 8.0,
     'cmp_pe_v': 4.69,
     'conv_b': 5.753,
     'mem_norm_g': 8.0,
     'mem_q_norm_g': 8.0,
     'mem_k_norm_g': 8.0,
     'ffn2_norm_g': 3.076,
     'attn_norm_g_2': 3.402,
     'shared_norm_g_2': 4.027,
     'shared_b_f_2': 5.988,
     'shared_k_norm_g_2': 8.0,
     'fox_q_norm_g_2': 8.0,
     'ple_norm_g_2': 46.756,
     'ffn_norm_g_2': 4.469}
    for name, (base, spread) in spreads.items():
        noise = np.random.default_rng([zlib.crc32(name.encode()), seed]).standard_normal(out[name].shape)
        drawn = base * np.exp(spread * noise) if base else spread * noise
        out[name] = __import__('jax').numpy.asarray(drawn.astype(out[name].dtype))
    for name, factor in factors.items():
        out[name] = (out[name] * factor).astype(out[name].dtype)
    return out
```

```python
from contextlib import ExitStack

import concourse.bass as bass
import numpy as np
from concourse import mybir

F32 = mybir.dt.float32
F32R = mybir.dt.float32r
ACT = mybir.ActivationFunctionType
ALU = mybir.AluOpType
AX = mybir.AxisListType

P = 128
D = 1024
S = 512
NCH = D // P
NTT = S // P
F = 2816
NF = F // P
NH = 16
HD = 64
NMEM = 256
MH = 4
NCMP = 31
NREL = 32
EPS = 1e-6
BIG = 1e30
HUGE = 3.0e38
K8, K11 = 8, 11
STRIP = 896
TAB = 1023

STREAM = [
    ("ffn0_in", 44, K8), ("ffn0_out", 16, K11),
    ("qkv0", 20, K8), ("memkv", 16, K8), ("qmem", 8, K8), ("gnsa", 8, K8), ("conv", 32, K8),
    ("gmem", 8, K8), ("wo0", 8, K8),
    ("ffn1_in", 44, K8), ("ffn1_out", 16, K11),
    ("sb_qkv", 24, K8), ("sb_o", 8, K8),
    ("ffn2_in", 44, K8), ("ffn2_out", 16, K11),
    ("ple0_proj", 2, K8), ("ple0_gate", 8, K8),
    ("fox_kv", 16, K8), ("fox_q", 8, K8), ("fox_o", 8, K8),
    ("ffn3_in", 44, K8), ("ffn3_out", 16, K11),
    ("ple1_proj", 2, K8), ("ple1_gate", 8, K8),
]


def stream_plan():
    first, tile, blocks, place = {}, {}, [], []
    t, n = 0, {K8: 0, K11: 0}
    for name, units, nk in STREAM:
        first[name], tile[name] = len(blocks), t
        t += units // 2 if name.endswith("_out") else units * 4 if name.endswith("_proj") else units
        for _ in range(units):
            blocks.append(nk)
            place.append(n[nk])
            n[nk] += 1
    return first, tile, blocks, place


U0, T0, BLOCKS, PLACE = stream_plan()
UNITS = {name: units for name, units, _ in STREAM}
NU = len(BLOCKS)

SPLITS = [("ffn0_norm", 8), ("ffn0", NF), ("mix_norm", 8), ("mem_norm", 8), ("gmem", 8),
          ("ffn1_norm", 8), ("ffn1", NF), ("attn0_norm", 8), ("ffn2_norm", 8), ("ffn2", NF),
          ("ple0_norm", 8), ("shared_norm", 8), ("attn1_norm", 8), ("ffn3_norm", 8), ("ffn3", NF),
          ("ple1_norm", 8)]
UPDATES = ["ffn0_out", "wo0", "ffn1_out", "sb_o", "ffn2_out", "ple0_gate", "fox_o", "ffn3_out", "ple1_gate"]
MEANS = ["ffn0", "mix", "mem", "ffn1", "attn0", "ffn2", "ple0", "shared", "ffn3", "ple1"]

VEC = {}
_at = 0
for _name, _n in [("ffn0", 8), ("mix", 8), ("ffn1", 8), ("attn0", 8), ("attn1", 8), ("shared", 8),
                  ("ffn2", 8), ("ffn3", 8), ("ple0", 8), ("ple1", 8), ("mem", 8), ("convw", 24), ("convb", 8),
                  ("qn", 1), ("kn", 1), ("mq", 2), ("mk", 2), ("shk", 1), ("fq", 1), ("pek", 32), ("pev", 32),
                  ("bf", 64), ("anyv", 4)]:
    VEC[_name] = _at
    _at += _n
NVEC = _at

CON = {}
_at = 0
for _name, _n in [("ident", 128), ("mean_d", 128), ("mean_head", 128), ("mean_mem", 128),
                  ("neg_tri", 128), ("neg_ones", 128), ("below", 128), ("cum", 512), ("causal", 512)]:
    CON[_name] = _at
    _at += _n
NCON = _at


def build(nc, w8, w11, x_t, mem_t, p_t, vec_d, con_d, wg_d, wf_d, cw1_d, cw2_d, rel_d, hot_d, aug_d, out_t):
    es = ExitStack()
    with es:
        def sb(name, shape, dt=F32, stack=es):
            return stack.enter_context(nc.sbuf_tensor(name, shape, dt))

        sems = {}

        def sem(name):
            if name not in sems:
                sems[name] = es.enter_context(nc.semaphore(name))
            return sems[name]

        x = sb("x", [P, NCH, S])
        a_hi = sb("a_hi", [P, NCH, S], F32R)
        a_lo = sb("a_lo", [P, NCH, S], F32R)
        raw = [sb(f"raw{i}", [P, K11 * P]) for i in range(4)]
        w_hi = [sb(f"w_hi{i}", [P, K11 * P], F32R) for i in range(2)]
        w_lo = [sb(f"w_lo{i}", [P, K11 * P], F32R) for i in range(2)]
        rstd = sb("rstd", [P, S])
        sqsum = sb("sqsum", [P, S])
        sqtmp = sb("sqtmp", [P, S])
        tmp = [sb(f"tmp{i}", [P, S]) for i in range(2)]
        act_t = [sb(f"act_t{i}", [P, S]) for i in range(2)]
        vec = sb("vec", [P, NVEC])
        con = sb("con", [P, NCON])
        vt = [sqtmp, sqsum]
        epsc = sb("epsc", [P, 1])
        stat = sb("stat", [P, 96])
        negq, negfq, negmq = sb("negq", [P, 1]), sb("negfq", [P, 1]), sb("negmq", [P, 2])
        mask_r = sb("mask_r", [P, P], F32R)
        ident_r = sb("ident_r", [P, P], F32R)

        def cst(name, n=P, p=P):
            return con[0:p, CON[name]:CON[name] + n]

        def vcol(name, k=0, n=1):
            return vec[:, VEC[name] + k:VEC[name] + k + n]

        ident = cst("ident")

        with ExitStack() as ph:
            hot = sb("hot", [33, 1024], F32, ph)
            rel = sb("rel", [33, NH], F32, ph)
            table = sb("table", [NH, 1024], F32, ph)
        with ExitStack() as ph:
            h_hi = sb("h_hi", [P, NF, S], F32R, ph)
            h_lo = sb("h_lo", [P, NF, S], F32R, ph)
        with ExitStack() as ph:
            q_t = sb("q_t", [P, NCH, S], F32, ph)
            with ExitStack() as ph2:
                cw1 = [sb(f"cw1{i}", [P, 8, 256], F32, ph2) for i in range(2)]
            mixed = sb("mixed", [P, NCH, S], F32, ph)
            with ExitStack() as ph2:
                kk = sb("kk", [P, 4, S], F32, ph2)
                vtok = sb("vtok", [P, 2, NTT, 256], F32, ph2)
                kcmp = sb("kcmp", [P, 2, 32], F32, ph2)
                vcmp = sb("vcmp", [32, 256], F32, ph2)
                gates = sb("gates", [P, NTT, 48], F32, ph2)
                with ExitStack() as ph3:
                    cc = sb("cc", [P, 2, 4, S], F32, ph3)
                    xc = sb("xc", [P, 16, 4, NCMP], F32, ph3)
                    cw2 = sb("cw2", [P, 2, 2, HD], F32, ph3)
                    chid = sb("chid", [P, 2, 4, NCMP], F32, ph3)
                    csq = sb("csq", [P, 2, 2 * NCMP], F32, ph3)
                    wg_raw = sb("wg_raw", [P, NCH * 48], F32, ph3)
                    wg_hi = sb("wg_hi", [P, NCH * 48], F32R, ph3)
                    wg_lo = sb("wg_lo", [P, NCH * 48], F32R, ph3)
                with ExitStack() as ph3:
                    strip = sb("strip", [P, 2, STRIP], F32, ph3)
                    q_st = sb("q_st", [P, S], F32, ph3)
                    prob = [sb(f"prob{i}", [P, 10 * P], F32, ph3) for i in range(2)]
                    prob_t = sb("prob_t", [P, NTT, S], F32, ph3)
                    cprob = sb("cprob", [P, 2, NTT, NCMP], F32, ph3)
                    cprob_t = sb("cprob_t", [32, S], F32, ph3)
            with ExitStack() as ph2:
                with ExitStack() as ph3:
                    memx = sb("memx", [P, NCH, NMEM], F32, ph3)
                    m_hi = sb("m_hi", [P, NCH, NMEM], F32R, ph3)
                    m_lo = sb("m_lo", [P, NCH, NMEM], F32R, ph3)
                with ExitStack() as ph3:
                    om = sb("om", [P, NCH, S], F32, ph3)
                    cu = sb("cu", [P, S + 2], F32, ph3)
                    cy = sb("cy", [P, S], F32, ph3)
                    cb = sb("cb", [P, S], F32, ph3)
                sb("phase_pad", [P, 3 * NCH * NMEM], F32, ph2)
                with ExitStack() as ph3:
                    km = sb("km", [P, NCH, NMEM], F32, ph3)
                    vm = sb("vm", [P, 2, D], F32, ph3)
                    mprob = [sb(f"mprob{i}", [P, NMEM], F32, ph3) for i in range(2)]
                    mprob_t = sb("mprob_t", [P, 2, S], F32, ph3)
                with ExitStack() as ph3:
                    b_hi = sb("b_hi", [P, NCH, S], F32R, ph3)
                    b_lo = sb("b_lo", [P, NCH, S], F32R, ph3)
        with ExitStack() as ph:
            q2 = sb("q2", [P, NCH, S], F32, ph)
            k2 = sb("k2", [P, NCH, S], F32, ph)
            v2 = sb("v2", [P, NTT, D], F32, ph)
            qs2 = sb("qs2", [P, S], F32, ph)
            ks2 = sb("ks2", [P, S], F32, ph)
            vs2 = sb("vs2", [P, NTT, P], F32, ph)
            with ExitStack() as ph2:
                sp = [sb(f"sp{i}", [P, 10 * P], F32, ph2) for i in range(2)]
                wt = [sb(f"wt{i}", [P, 10 * P], F32, ph2) for i in range(2)]
            with ExitStack() as ph2:
                fprob = [sb(f"fprob{i}", [P, 10 * P], F32, ph2) for i in range(2)]
                fprob_t = sb("fprob_t", [P, NTT, S], F32, ph2)
                augq = sb("augq", [2, 2, S], F32, ph2)
                augk = sb("augk", [2, 2, S], F32, ph2)
                wf_raw = sb("wf_raw", [P, NCH * NH], F32, ph2)
                wf_hi = sb("wf_hi", [P, NCH * NH], F32R, ph2)
                wf_lo = sb("wf_lo", [P, NCH * NH], F32R, ph2)
                fl = sb("fl", [P, 3, NTT * NH], F32, ph2)
                fcum = sb("fcum", [NH, S], F32, ph2)
        with ExitStack() as ph:
            p_raw = sb("p_raw", [P, 2, S], F32, ph)
            p_hi = sb("p_hi", [P, 2, S], F32R, ph)
            p_lo = sb("p_lo", [P, 2, S], F32R, ph)
            proj = sb("proj", [P, NCH, S], F32, ph)

        table_d = nc.dram_tensor("bias_table", [NH, 1024], F32)
        rows_d = nc.dram_tensor("bias_rows", [NH, P * 1024], F32)
        fcum_d = nc.dram_tensor("forget_cumsum", [NH, S], F32)

        bank = [es.enter_context(nc.psum_tensor(f"bank{i}", [P, 512], F32)) for i in range(8)]
        block = es.enter_context(nc.Block())

        def loop(eng, a, b, body):
            if b - a >= 2:
                with eng.Fori(a, b) as i:
                    body(i)
            elif b > a:
                body(a)

        def groups(eng, name, per, body, ahead=0):
            u, n = U0[name], UNITS[name]
            its = n // per
            alone = ahead and (u + n + ahead > NU or BLOCKS[u + n] != BLOCKS[u])
            if alone:
                loop(eng, 0, its - 1, body)
                body(its - 1)
            else:
                loop(eng, 0, its, body)

        def col(t, c):
            return t[:, bass.ds(c, 1), :].rearrange("p a n -> p (a n)")

        class Link:

            def __init__(self, eng, name):
                self.eng, self.sem, self.n, self.off = eng, sem(name), 0, 0

            def __call__(self, ins):
                self.n += 1
                ins.then_inc(self.sem, 1)
                self.eng.wait_ge(self.sem, self.off + self.n)

            def loop(self, a, b, per, body, run=None):
                start = self.n

                def counted(i):
                    self.n, self.off = start, i * per
                    body(i)
                    assert self.n - start == per, (self.n - start, per)
                (run or (lambda f: loop(self.eng, a, b, f)))(counted)
                self.n, self.off = start + (b - a) * per, 0

        split_base = {}
        q = 0
        for nm, n in SPLITS:
            split_base[nm] = q
            q += n

        tiles = {
            "qkv0": [("norm", q_t[:, c, :], negq[:, 0:1], "mean_head", 1) for c in range(8)]
            + [("cc", cc, 0, 0), ("cc", cc, 0, 1), ("cc", cc, 1, 0), ("cc", cc, 1, 1)]
            + [("norm", kk[:, c, :], vcol("kn"), "mean_head", 1) for c in range(2)]
            + [("v", vtok[:, 0], c) for c in range(2)]
            + [("norm", kk[:, 2 + c, :], vcol("kn"), "mean_head", 1) for c in range(2)]
            + [("v", vtok[:, 1], c) for c in range(2)],
            "memkv": [("norm", km[:, c, :], vcol("mk", c % 2), "mean_mem", 2) for c in range(8)]
            + [("v", vm, c) for c in range(8)],
            "qmem": [("norm", q_t[:, c, :], negmq[:, c % 2:c % 2 + 1], "mean_mem", 2) for c in range(8)],
            "sb_qkv": [("plain", q2[:, c, :], HD ** -0.5) for c in range(8)]
            + [("plain", k2[:, c, :], 1.0) for c in range(8)] + [("v", v2, c) for c in range(8)],
            "fox_kv": [("norm", k2[:, c, :], vcol("shk"), "mean_head", 1) for c in range(8)]
            + [("v", v2, c) for c in range(8)],
            "fox_q": [("norm", q2[:, c, :], negfq[:, 0:1], "mean_head", 1) for c in range(8)],
        }
        norm0, sq0, v0, g, n, v = {}, {}, {}, 0, 0, 0
        for nm in tiles:
            norm0[nm], sq0[nm], v0[nm] = g, n, v
            g += sum(1 / t[4] for t in tiles[nm] if t[0] == "norm")
            n += sum(t[0] == "norm" for t in tiles[nm])
            v += sum(t[0] == "v" for t in tiles[nm])
            g = int(g)
        taken0, n = {}, 4
        for nm, units, nk in STREAM:
            taken0[nm] = n
            if nm in tiles or nm in ("gnsa", "conv", "gmem"):
                n += units
            if nm.endswith("_proj"):
                n += 8

        gates0 = {"gnsa": 0, "gmem": 8, "ple0_gate": 16, "ple1_gate": 24}
        x0 = {nm: 4 + 8 * n for n, nm in enumerate(UPDATES)}
        mean_no = {nm: n for n, nm in enumerate(MEANS)}
        items = [(0, 0, 512), (1, 0, 384), (2, 0, 256), (1, 384, 128)]
        z_ops = [(0, 0, 512), (1, 512, 512), (2, 1024, 256)]
        z_at = [0, 512, 1024, 896]
        p_at = [0, 128, 384, 768]

        @block.sync
        def _(eng):
            def load(u, i, k, per=4):
                v, nk = u + k, BLOCKS[u + k]
                if not (isinstance(i, int) and v + 4 * i < 4):
                    eng.wait_ge(sem("w_lo_ready"), 4 * i + v - 3)
                src = (w8 if nk == K8 else w11)[bass.ds(PLACE[v] + 4 * i, 1)]
                eng.dma_start(raw[v % 4][:, 0:nk * P], src.rearrange("a p n -> p (a n)"))\
                   .then_inc(sem(f"w_raw{v % 4}"), 16)

            u = 0
            while u < NU:
                n = 1
                while u + n < NU and BLOCKS[u + n] == BLOCKS[u]:
                    n += 1
                head = 4 if u == 0 else 0
                for k in range(head):
                    load(u, 0, k)
                its = (n - head) // 4

                def body(i, u=u + head):
                    for k in range(4):
                        load(u, i, k)
                loop(eng, 0, its, body)
                for v in range(u + head + 4 * its, u + n):
                    load(v, 0, 0)
                u += n
            eng.wait_ge(sem("x_done"), 4 + 8 * len(UPDATES))
            eng.dma_start(out_t, x[:, :, :]).then_inc(sem("out_stored"), 16)
            eng.wait_ge(sem("out_stored"), 16)

        @block.tensor
        def _(eng):
            mm = eng.matmul

            def unit(u, off, dst, hi, lo, nk, start=True, stop=True, kbase=0, w0=0):
                s = u % 2
                eng.wait_ge(sem("w_lo_ready"), u + off + 1)
                for b in range(nk):
                    w = slice((w0 + b) * P, (w0 + b + 1) * P)
                    mm(dst, w_hi[s][:, w], hi[:, kbase + b], start=start and b == 0, stop=False)
                    mm(dst, w_lo[s][:, w], hi[:, kbase + b], start=False, stop=False)
                    last = mm(dst, w_hi[s][:, w], lo[:, kbase + b], start=False, stop=stop and b == nk - 1)
                return last

            def mean(name, n=S):
                eng.wait_ge(sem("sqsum_done"), mean_no[name] + 1)
                mm(bank[4][:, 0:n], cst("mean_d"), sqsum[:, 0:n], start=True, stop=True)\
                    .then_inc(sem("mean_done"), 1)

            def ffn(f, name):
                mean(f"ffn{f}")
                eng.wait_ge(sem("lo_done"), 2 + split_base[f"ffn{f}_norm"] + 8)
                u, q = U0[f"ffn{f}_in"], split_base[f"ffn{f}"]

                def body(i):
                    for k in range(4):
                        eng.wait_ge(sem("tmp_ready"), q + 2 * i + k // 2 - 1)
                        unit(u + k, 4 * i, bank[k][:, :], a_hi, a_lo, K8).then_inc(sem("unit_done"), 1)
                groups(eng, f"ffn{f}_in", 4, body)
                eng.wait_ge(sem("lo_done"), 2 + q + NF)
                v, xb = U0[f"ffn{f}_out"], x0[f"ffn{f}_out"]

                def body(i):
                    for k in range(4):
                        eng.wait_ge(sem("x_done"), xb + 4 * i + k - 3)
                        unit(v + 2 * k, 8 * i, bank[k][:, :], h_hi, h_lo, K11, stop=False)\
                            .then_inc(sem("unit_done"), 1)
                        unit(v + 2 * k + 1, 8 * i, bank[k][:, :], h_hi, h_lo, K11, start=False, kbase=K11)\
                            .then_inc(sem("unit_done"), 1)
                groups(eng, f"ffn{f}_out", 8, body)

            def project(name, hi, lo, n=S):
                u, ts = U0[name], tiles[name]
                g, vn = norm0[name], v0[name]
                pending, group = [], []

                def post():
                    nonlocal g, vn
                    while pending:
                        kind, t, sq = pending.pop(0)
                        if kind == "norm":
                            size = ts[t][4]
                            if g >= 2:
                                eng.wait_ge(sem("root_done"), g - 1)
                            eng.wait_ge(sem("square_ready"), sq + 1)
                            for j in range(size):
                                last = mm(bank[4 + g % 2][:, 0:n], cst(ts[t][3]), act_t[(sq + 1 - size + j) % 2][:, 0:n],
                                          start=j == 0, stop=j == size - 1)
                            last.then_inc(sem("head_mean"), 1)
                            g += 1
                        else:
                            eng.wait_ge(sem("tile_taken"), taken0[name] + t + 1)
                            if vn >= 2:
                                eng.wait_ge(sem("vtok_done"), vn - 1)
                            for j in range(n // P):
                                last = eng.transpose(bank[6 + vn % 2][:, j * P:(j + 1) * P],
                                                     vt[vn % 2][:, j * P:(j + 1) * P], ident)
                            last.then_inc(sem("v_turned"), 1)
                            vn += 1

                sq = sq0[name]
                for t, tile in enumerate(ts):
                    eng.wait_ge(sem("tile_taken"), taken0[name] + t - 3)
                    last = unit(u + t, 0, bank[t % 4][:, 0:n], hi, lo, K8)
                    last.then_inc(sem("unit_done"), 1)
                    post()
                    if tile[0] == "norm":
                        sq += 1
                        if (sq - sq0[name]) % tile[4] == 0:
                            pending.append(("norm", t, sq - 1))
                    elif tile[0] == "v":
                        pending.append(("v", t, 0))
                post()

            def small(vtotal, w_hi_s, w_lo_s, n, ready, done):
                eng.wait_ge(sem(ready), 1)
                eng.wait_ge(sem("vtok_done"), vtotal)
                for tt in range(NTT):
                    t = slice(tt * P, (tt + 1) * P)
                    for b in range(NCH):
                        w = slice(b * n, (b + 1) * n)
                        mm(bank[7][:, tt * n:(tt + 1) * n], a_hi[:, b, t], w_hi_s[:, w], start=b == 0, stop=False)
                        mm(bank[7][:, tt * n:(tt + 1) * n], a_hi[:, b, t], w_lo_s[:, w], start=False, stop=False)
                        last = mm(bank[7][:, tt * n:(tt + 1) * n], a_lo[:, b, t], w_hi_s[:, w],
                                  start=False, stop=b == NCH - 1)
                last.then_inc(sem(done), 1)

            def compress():
                eng.wait_ge(sem("root_done"), norm0["memkv"])
                eng.wait_ge(sem("gates_ready"), 1)
                for kv in range(2):
                    eng.wait_ge(sem("xc_ready"), kv + 1)
                    for half in range(2):
                        eng.wait_ge(sem(f"cw1_in{half}"), 16 * kv + 16)
                        for ht in range(2):
                            if half == 0 and kv == 1:
                                eng.wait_ge(sem("chid_ready"), 2)
                            for j in range(8):
                                last = mm(bank[4 + ht][:, 0:4 * NCMP], cw1[half][:, j, ht * P:(ht + 1) * P],
                                          xc[:, 8 * half + j], start=half == 0 and j == 0,
                                          stop=half == 1 and j == 7)
                        last.then_inc(sem("cw1_used"), 1)
                    eng.wait_ge(sem("chid_ready"), 2 * kv + 2)
                    if kv == 0:
                        eng.wait_ge(sem("cw2_in"), 16)
                        for par in range(2):
                            for ht in range(2):
                                last = mm(bank[6][64 * par:64 * par + 64, 0:2 * NCMP], cw2[:, 0, ht, :],
                                          chid[:, ht, par::2, :], start=ht == 0, stop=ht == 1)
                        last.then_inc(sem("kcmp_raw"), 1)
                        eng.wait_ge(sem("ksq_ready"), 1)
                        mm(bank[7][:, 0:2 * NCMP], cst("mean_head"), csq[:, 0, :], start=True, stop=True)\
                            .then_inc(sem("kcmp_mean"), 1)
                    else:
                        eng.wait_ge(sem("kcmp_done"), 1)
                        for g in range(4):
                            for ht in range(2):
                                last = mm(bank[6][0:NCMP, g * HD:(g + 1) * HD], chid[:, ht, g, :], cw2[:, 1, ht, :],
                                          start=ht == 0, stop=ht == 1)
                        last.then_inc(sem("vcmp_raw"), 1)

            def bias_table():
                eng.wait_ge(sem("rel_in"), 32)
                for h in range(2):
                    last = mm(bank[6 + h][0:NH, :], rel[:, :], hot[:, h * 512:(h + 1) * 512], start=True, stop=True)
                last.then_inc(sem("table_raw"), 1)

            def full_scores(q, k, i4, par, n, pre, aug=False):
                for i in range(4):
                    eng.wait_ge(sem(pre + "biased"), i4 + 4 * n + i - 4 + 4 + 1)
                    w = (i + 1) * P
                    r = slice(64 * par, 64 * par + 64)
                    last = mm(bank[i][:, 0:w], q[r, i * P:(i + 1) * P], k[r, 0:w], start=True, stop=not aug)
                    if aug:
                        last = mm(bank[i][:, 0:w], augq[:, par, i * P:(i + 1) * P], augk[:, par, 0:w],
                                  start=False, stop=True)
                    last.then_inc(sem(pre + "scored"), 1)

            def turn(pb, i4, n, pre):
                for i in range(4):
                    eng.wait_ge(sem(pre + "scaled"), i4 + 4 * n + i + 1)
                    eng.wait_ge(sem(pre + "copied"), i4 + 4 * n + i + 1)
                    for j in range(i + 1):
                        last = eng.transpose(bank[4 + i % 2][:, j * P:(j + 1) * P],
                                             pb[:, p_at[i] + j * P:p_at[i] + (j + 1) * P], ident)
                    last.then_inc(sem(pre + "turned"), 1)

            def values(v, pt, i4, n, par, pre, start, stop):
                eng.wait_ge(sem(pre + "copied"), i4 + 4 * n + 4 + 2)
                for j in range(4):
                    last = mm(bank[7][64 * par:64 * par + 64, j * P:S], v(j), pt[:, j, j * P:S],
                              start=start and j == 0, stop=stop and j == 3, skip_group_check=True)
                last.then_inc(sem(pre + "valued"), 1)

            def nsa():
                for name in ("n_scored", "n_valued", "n_cvalued"):
                    eng.sem_inc(sem(name), 1)
                eng.wait_ge(sem("kcmp_done"), 1)
                for a in range(2):
                    def body(r, a=a):
                        c = 4 * a + r
                        eng.wait_ge(sem("q_staged"), c + 1)

                        def cmp_scores(par):
                            if par == 0:
                                eng.wait_ge(sem("n_cadded"), 2 * c + 1)
                            else:
                                eng.wait_ge(sem("n_cadded"), 2 * c + 2)
                            for i in range(4):
                                last = mm(bank[6][:, i * 32:i * 32 + NCMP], q_st[64 * par:64 * par + 64, i * P:(i + 1) * P],
                                          kcmp[64 * par:64 * par + 64, a, 0:NCMP], start=True, stop=True)
                            last.then_inc(sem("n_cscored"), 1)

                        def cmp_values(par):
                            eng.wait_ge(sem("n_cscaled"), 2 * c + par + 1)
                            eng.wait_ge(sem("n_copied"), 16 * c + (0, 8)[par] + 2)
                            for i in range(4):
                                last = eng.transpose(bank[4][0:NCMP, i * P:(i + 1) * P], cprob[:, par, i, :], ident)
                            last.then_inc(sem("n_cturned"), 1)
                            eng.wait_ge(sem("n_ccopied"), 2 * c + par + 1)
                            if par == 0:
                                eng.wait_ge(sem("n_out_taken"), c + 1)
                            g = 2 * a + par
                            mm(bank[7][64 * par:64 * par + 64, :], vcmp[0:NCMP, g * HD:(g + 1) * HD], cprob_t[0:NCMP, :],
                               start=True, stop=False, skip_group_check=True).then_inc(sem("n_cvalued"), 1)

                        def scores(n):
                            full_scores(q_st, kk[:, 2 * (n % 2) + a, :], 16 * c, n // 2, n, "n_")

                        def turned(n):
                            turn(prob[n % 2], 16 * c, n, "n_")

                        def valued(n):
                            g = 2 * a + n // 2
                            values(lambda j: vtok[:, n % 2, j, g * HD:(g + 1) * HD], prob_t, 16 * c, n, n // 2, "n_",
                                   False, n % 2 == 1)

                        cmp_scores(0)
                        scores(0)
                        scores(1)
                        cmp_scores(1)
                        cmp_values(0)
                        turned(0)
                        scores(2)
                        valued(0)
                        turned(1)
                        scores(3)
                        valued(1)
                        cmp_values(1)
                        turned(2)
                        valued(2)
                        turned(3)
                        valued(3)
                    loop(eng, 0, 4, body)

            def mem_attention():
                for mh in range(MH):
                    par, a = mh % 2, mh // 2
                    for i in range(4):
                        t = 4 * mh + i
                        if t >= 2:
                            eng.wait_ge(sem("m_exped"), t - 1)
                        for kc in range(2):
                            last = mm(bank[4 + t % 2][:, 0:NMEM], q_t[:, 2 * mh + kc, i * P:(i + 1) * P],
                                      km[:, 2 * mh + kc, :], start=kc == 0, stop=kc == 1)
                        last.then_inc(sem("m_scored"), 1)
                        if t >= 1:
                            mem_turn(t - 1)
                        if t >= 4 and i == 1:
                            mem_values(mh - 1)
                mem_turn(4 * MH - 1)
                mem_values(MH - 1)

            def mem_turn(t):
                eng.wait_ge(sem("m_scaled"), t + 1)
                if t >= 2:
                    eng.wait_ge(sem("m_copied"), t - 1)
                for kt in range(2):
                    last = eng.transpose(bank[6 + t % 2][:, kt * P:(kt + 1) * P], mprob[t % 2][:, kt * P:(kt + 1) * P], ident)
                last.then_inc(sem("m_turned"), 1)

            def mem_values(mh):
                par, a = mh % 2, mh // 2
                eng.wait_ge(sem("m_copied"), 4 * mh + 4)
                if mh == 2:
                    eng.wait_ge(sem("m_out_taken"), 4)
                for r in range(4):
                    for kt in range(2):
                        last = mm(bank[r][64 * par:64 * par + 64, :], vm[:, kt, mh * 256 + r * HD:mh * 256 + (r + 1) * HD],
                                  mprob_t[:, kt, :], start=kt == 0, stop=kt == 1, skip_group_check=True)
                last.then_inc(sem("m_valued"), 1)

            def tiles_by_four(name, hi, lo, count, base):
                u = U0[name]

                def body(i):
                    for k in range(4):
                        eng.wait_ge(sem(count), base + 4 * i + k - 3)
                        unit(u + k, 4 * i, bank[k][:, :], hi, lo, K8).then_inc(sem("unit_done"), 1)
                groups(eng, name, 4, body)

            def stick_breaking():
                for name in ("s_z", "s_valued"):
                    eng.sem_inc(sem(name), 1)
                sp_t = [[sp[p][:, z_at[j]:z_at[j] + S - j * P] for j in range(4)] for p in range(2)]
                wt_t = [[wt[p][:, z_at[j]:z_at[j] + S - j * P] for j in range(4)] for p in range(2)]

                def z(p, j):
                    b, at, w = items[j]
                    return bank[3 * p + b][:, at:at + w]

                def body(c):
                    eng.wait_ge(sem("s_staged"), c + 1)
                    eng.wait_ge(sem("s_exped"), 2 * c + 1)
                    for p in range(2):
                        if p:
                            eng.wait_ge(sem("s_exped"), 2 * c + 2)
                        r = slice(64 * p, 64 * p + 64)
                        for j in range(4):
                            mm(z(p, j), ks2[r, j * P:(j + 1) * P], qs2[r, j * P:S], start=j < 3, stop=False,
                               skip_group_check=True)
                            last = mm(z(p, j)[:, 0:P], mask_r[:, :], ident_r[:, :], start=False, stop=False,
                                      skip_group_check=True)
                        last.then_inc(sem("s_z"), 1)
                    for p in range(2):
                        eng.wait_ge(sem("s_soft"), 2 * c + p + 1)
                        for j in range(4):
                            for jj in range(j, 4):
                                last = mm(z(p, j)[:, (jj - j) * P:S - j * P], cst("neg_tri" if jj == j else "neg_ones"),
                                          sp_t[p][jj], start=False, stop=jj == 3, skip_group_check=True)
                        last.then_inc(sem("s_summed"), 1)
                    for p in range(2):
                        eng.wait_ge(sem("s_exped"), 2 * c + p + 3)
                        if p == 0:
                            eng.wait_ge(sem("s_out_taken"), c + 1)
                        for j in range(4):
                            last = mm(bank[6][64 * p:64 * p + 64, j * P:S], vs2[:, j, 64 * p:64 * p + 64], wt_t[p][j],
                                      start=j == 0, stop=j == 3, skip_group_check=True)
                        last.then_inc(sem("s_valued"), 1)
                loop(eng, 0, 8, body)

            def forget_cumsum():
                eng.wait_ge(sem("log_f"), 1)
                for tt in range(NTT):
                    last = mm(bank[7][0:NH, tt * P:S], fl[:, 1, tt * NH:(tt + 1) * NH], cst("cum", S - tt * P),
                              start=tt == 0, stop=tt == NTT - 1, skip_group_check=True)
                last.then_inc(sem("fcum_raw"), 1)

            def forgetting():
                for name in ("f_scored", "f_valued"):
                    eng.sem_inc(sem(name), 1)

                def body(c):
                    eng.wait_ge(sem("f_staged"), c + 1)
                    eng.wait_ge(sem("f_aug"), 32 * c + 64)
                    full_scores(qs2, ks2, 8 * c, 0, 0, "f_", True)
                    full_scores(qs2, ks2, 8 * c, 1, 1, "f_", True)
                    for n in range(2):
                        turn(fprob[n], 8 * c, n, "f_")
                        if n == 0:
                            eng.wait_ge(sem("f_out_taken"), c + 1)
                        values(lambda j: vs2[:, j, 64 * n:64 * n + 64], fprob_t, 8 * c, n, n, "f_", True, True)
                loop(eng, 0, 8, body)

            def ple(n):
                name = f"ple{n}"
                mean(name)
                u = U0[name + "_proj"]
                eng.wait_ge(sem("p_split"), n + 1)
                for t in range(8):
                    eng.wait_ge(sem("tile_taken"), taken0[name + "_proj"] + t - 3)
                    last = unit(u + t // 4, 0, bank[t % 4][:, :], p_hi, p_lo, 2, w0=2 * (t % 4))
                    if t % 4 == 3:
                        last.then_inc(sem("unit_done"), 1)
                eng.wait_ge(sem("tile_taken"), taken0[name + "_proj"] + 8)
                eng.wait_ge(sem("lo_done"), 2 + split_base[name + "_norm"] + 8)
                tiles_by_four(name + "_gate", a_hi, a_lo, "x_done", x0[name + "_gate"])

            bias_table()
            eng.wait_ge(sem("const_in"), 16)
            ffn(0, "ffn0")
            mean("mix")
            eng.wait_ge(sem("lo_done"), 2 + split_base["mix_norm"] + 8)
            project("qkv0", a_hi, a_lo)
            small(v0["memkv"], wg_hi, wg_lo, 48, "wg_split", "gates_raw")
            compress()
            nsa()
            mean("mem", NMEM)
            eng.wait_ge(sem("lo_done"), 2 + split_base["mem_norm"] + 8)
            eng.wait_ge(sem("n_out_taken"), 9)
            project("memkv", m_hi, m_lo, NMEM)
            project("qmem", a_hi, a_lo)
            eng.wait_ge(sem("tile_taken"), taken0["gnsa"])
            mem_attention()
            eng.wait_ge(sem("m_out_taken"), 8)
            tiles_by_four("gnsa", a_hi, a_lo, "tile_taken", taken0["gnsa"])
            tiles_by_four("conv", a_hi, a_lo, "tile_taken", taken0["conv"])
            tiles_by_four("gmem", a_hi, a_lo, "tile_taken", taken0["gmem"])
            eng.wait_ge(sem("lo_done"), 2 + split_base["gmem"] + 8)
            tiles_by_four("wo0", b_hi, b_lo, "x_done", x0["wo0"])
            ffn(1, "ffn1")
            mean("attn0")
            eng.wait_ge(sem("lo_done"), 2 + split_base["attn0_norm"] + 8)
            project("sb_qkv", a_hi, a_lo)
            stick_breaking()
            eng.wait_ge(sem("s_out_taken"), 9)
            tiles_by_four("sb_o", a_hi, a_lo, "x_done", x0["sb_o"])
            ffn(2, "ffn2")
            ple(0)
            mean("shared")
            eng.wait_ge(sem("lo_done"), 2 + split_base["shared_norm"] + 8)
            project("fox_kv", a_hi, a_lo)
            small(v0["fox_q"], wf_hi, wf_lo, NH, "wf_split", "f_raw")
            forget_cumsum()
            eng.wait_ge(sem("lo_done"), 2 + split_base["attn1_norm"] + 8)
            project("fox_q", a_hi, a_lo)
            forgetting()
            eng.wait_ge(sem("f_out_taken"), 9)
            tiles_by_four("fox_o", a_hi, a_lo, "x_done", x0["fox_o"])
            ffn(3, "ffn3")
            ple(1)

        @block.scalar
        def _(eng):
            act = eng.activation
            own = Link(eng, "scalar_step")

            def split(v, i, per):
                nk = BLOCKS[v]
                eng.wait_ge(sem(f"w_raw{v % 4}"), 16 * (v // 4 + 1) + i * (per * 4))
                if v >= 2:
                    eng.wait_ge(sem("unit_done"), v - 1 + i * per)
                act(w_hi[v % 2][:, 0:nk * P], raw[v % 4][:, 0:nk * P], ACT.Copy).then_inc(sem("w_hi_ready"), 1)

            def ahead(name, i, k, per):
                v = U0[name] + k + 2
                if isinstance(i, int):
                    v += i * per
                    if v < NU:
                        split(v, 0, per)
                else:
                    split(v, i, per)

            def root(name, n=S):
                eng.wait_ge(sem("mean_done"), mean_no[name] + 1)
                own(act(rstd[:, 0:n], bank[4][:, 0:n], ACT.Ln, bias=epsc[:, 0:1]))
                act(rstd[:, 0:n], rstd[:, 0:n], ACT.Exp, scale=-0.5).then_inc(sem("rstd_ready"), 1)

            def high_parts(name, hi, n=S):
                q = split_base[name]
                for k in range(NCH):
                    eng.wait_ge(sem("tmp_ready"), q + k + 1)
                    act(hi[:, k, :], tmp[k % 2][:, 0:n], ACT.Copy).then_inc(sem("hi_done"), 1)

            def norm(name, hi, n=S, mean=True):
                if mean:
                    root(name, n)
                high_parts(f"{name}_norm", hi, n)

            def ffn(f):
                norm(f"ffn{f}", a_hi)
                u, q = U0[f"ffn{f}_in"], split_base[f"ffn{f}"]

                def body(i):
                    for k in range(4):
                        ahead(f"ffn{f}_in", i, k, 4)
                        if k % 2 == 0:
                            eng.wait_ge(sem("unit_done"), u + 4 * i + k + 1)
                            eng.wait_ge(sem("tmp_ready"), q + 2 * i + k // 2 - 1)
                            act(act_t[k // 2][:, :], bank[k][:, :], ACT.Silu).then_inc(sem("silu_done"), 1)
                        else:
                            h = 2 * i + k // 2
                            eng.wait_ge(sem("tmp_ready"), q + h + 1)
                            act(col(h_hi, h), tmp[k // 2][:, :], ACT.Copy).then_inc(sem("hi_done"), 1)
                groups(eng, f"ffn{f}_in", 4, body, 2)

                def body(i):
                    for k in range(8):
                        ahead(f"ffn{f}_out", i, k, 8)
                groups(eng, f"ffn{f}_out", 8, body, 2)

            def project(name, n=S):
                u, ts, g, vn, sq = U0[name], tiles[name], norm0[name], v0[name], sq0[name]
                pending, ended = [], []

                def post():
                    nonlocal g, vn
                    while pending:
                        kind, t = pending.pop(0)
                        if kind == "norm":
                            eng.wait_ge(sem("head_mean"), g + 1)
                            if len(ended) >= 2:
                                eng.wait_ge(sem("tile_taken"), taken0[name] + ended[-2] + 1)
                            ended.append(t)
                            own(act(tmp[g % 2][:, 0:n], bank[4 + g % 2][:, 0:n], ACT.Ln, bias=epsc[:, 0:1]))
                            act(tmp[g % 2][:, 0:n], tmp[g % 2][:, 0:n], ACT.Exp, scale=-0.5).then_inc(sem("root_done"), 1)
                            g += 1
                        else:
                            eng.wait_ge(sem("v_turned"), vn + 1)
                            dst, c = ts[t][1], ts[t][2]
                            act(dst[:, 0:n // P, c * P:(c + 1) * P],
                                bank[6 + vn % 2][:, 0:n].rearrange("p (t n) -> p t n", n=P), ACT.Copy)\
                                .then_inc(sem("vtok_done"), 1)
                            vn += 1

                for t, tile in enumerate(ts):
                    ahead(name, 0, t, 4)
                    if tile[0] == "norm":
                        need = g + sum(kind == "norm" for kind, _ in pending) - (1 if tile[4] == 1 else 0)
                        if need >= 1:
                            eng.wait_ge(sem("head_mean"), need)
                        eng.wait_ge(sem("unit_done"), u + t + 1)
                        act(act_t[sq % 2][:, 0:n], bank[t % 4][:, 0:n], ACT.Square).then_inc(sem("square_ready"), 1)
                        sq += 1
                    post()
                    if tile[0] == "norm" and (sq - sq0[name]) % tile[4] == 0:
                        pending.append(("norm", t))
                    elif tile[0] == "v":
                        pending.append(("v", t))
                post()

            def exps(pb, i4, n, pre, slot):
                for i in range(4):
                    eng.wait_ge(sem(pre + "biased"), i4 + 4 * n + i + 1 + 4)
                    w = (i + 1) * P
                    act(pb[:, p_at[i]:p_at[i] + w], pb[:, p_at[i]:p_at[i] + w], ACT.Exp, scale=-1.0,
                        bias=stat[:, 4 * slot + i:4 * slot + i + 1],
                        accum_out=stat[:, 8 + 4 * slot + i:9 + 4 * slot + i]).then_inc(sem(pre + "exped"), 1)

            def copies(pt, i4, f, n, pre):
                for i in range(4):
                    eng.wait_ge(sem(pre + "turned"), i4 + 4 * n + i + 1)
                    eng.wait_ge(sem(pre + "valued"), f + n + 1)
                    act(pt[:, 0:i + 1, i * P:(i + 1) * P],
                        bank[4 + i % 2][:, 0:(i + 1) * P].rearrange("p (j n) -> p j n", n=P), ACT.Copy)\
                        .then_inc(sem(pre + "copied"), 1)

            def nsa():
                for a in range(2):
                    def body(r, a=a):
                        c = 4 * a + r

                        def cexp(par):
                            eng.wait_ge(sem("n_cmin"), 2 * c + par + 1)
                            act(cprob[:, par], cprob[:, par], ACT.Exp, scale=-1.0).then_inc(sem("n_cexped"), 1)

                        def ccopy(par):
                            eng.wait_ge(sem("n_cturned"), 2 * c + par + 1)
                            eng.wait_ge(sem("n_cvalued"), 2 * c + par + 1)
                            act(cprob_t[0:NCMP, :], bank[4][0:NCMP, :], ACT.Copy).then_inc(sem("n_ccopied"), 1)

                        cexp(0)
                        exps(prob[0], 16 * c, 0, "n_", 0)
                        exps(prob[1], 16 * c, 1, "n_", 1)
                        cexp(1)
                        ccopy(0)
                        copies(prob_t, 16 * c, 4 * c, 0, "n_")
                        exps(prob[0], 16 * c, 2, "n_", 0)
                        copies(prob_t, 16 * c, 4 * c, 1, "n_")
                        exps(prob[1], 16 * c, 3, "n_", 1)
                        ccopy(1)
                        copies(prob_t, 16 * c, 4 * c, 2, "n_")
                        copies(prob_t, 16 * c, 4 * c, 3, "n_")
                    loop(eng, 0, 4, body)

            def mem_attention():
                def exp(t):
                    eng.wait_ge(sem("m_min"), t + 1)
                    if t >= 2:
                        eng.wait_ge(sem("m_turned"), t - 1)
                    act(mprob[t % 2][:, :], bank[4 + t % 2][:, 0:NMEM], ACT.Exp, scale=-1.0, bias=stat[:, t:t + 1],
                        accum_out=stat[:, 16 + t:17 + t]).then_inc(sem("m_exped"), 1)

                def copy(t):
                    eng.wait_ge(sem("m_turned"), t + 1)
                    if t >= 4:
                        eng.wait_ge(sem("m_valued"), t // 4)
                    i = t % 4
                    act(mprob_t[:, :, i * P:(i + 1) * P], bank[6 + t % 2][:, 0:NMEM].rearrange("p (k n) -> p k n", n=P),
                        ACT.Copy).then_inc(sem("m_copied"), 1)
                for t in range(4 * MH):
                    exp(t)
                    if t:
                        copy(t - 1)
                copy(4 * MH - 1)

            def gate_tiles(name, count, base, high=None):
                u = U0[name]

                def high_part(i, k):
                    eng.wait_ge(sem("tmp_ready"), base + 4 * i + k + 1)
                    act(col(high, 4 * i + k), tmp[k % 2][:, :], ACT.Copy).then_inc(sem("hi_done"), 1)

                def body(i):
                    for k in range(4):
                        ahead(name, i, k, 4)
                        eng.wait_ge(sem("unit_done"), u + 4 * i + k + 1)
                        eng.wait_ge(sem(count), base + 4 * i + k - 1)
                        act(act_t[k % 2][:, :], bank[k][:, :], ACT.Sigmoid).then_inc(sem("sigmoid_done"), 1)
                        if high is not None and k:
                            high_part(i, k - 1)
                    if high is not None:
                        high_part(i, 3)
                groups(eng, name, 4, body, 2)

            def conv():
                u = U0["conv"]

                def body(i):
                    for k in range(4):
                        ahead("conv", i, k, 4)
                        if k == 0:
                            eng.wait_ge(sem("unit_done"), u + 4 * i + 1)
                            eng.wait_ge(sem("tile_taken"), taken0["conv"] + 4 * i)
                            act(cb[:, :], bank[0][:, :], ACT.Copy).then_inc(sem("gates_copied"), 1)
                        if k == 1:
                            eng.wait_ge(sem("unit_done"), u + 4 * i + 2)
                            act(act_t[0][:, :], bank[1][:, :], ACT.Copy).then_inc(sem("gates_copied"), 1)
                        if k == 3:
                            eng.wait_ge(sem("unit_done"), u + 4 * i + 4)
                            act(act_t[1][:, :], bank[3][:, :], ACT.Sigmoid).then_inc(sem("sigmoid_conv"), 1)
                groups(eng, "conv", 4, body, 2)

            def stick_breaking():
                def body(c):
                    for p in range(2):
                        for o, (b, at, w) in enumerate(z_ops):
                            eng.wait_ge(sem("s_min"), 6 * c + 3 * p + o + 1)
                            own(act(sp[p][:, at:at + w], sp[p][:, at:at + w], ACT.Exp))
                            act(sp[p][:, at:at + w], sp[p][:, at:at + w], ACT.Ln, bias=1.0).then_inc(sem("s_log"), 1)
                    for p in range(2):
                        eng.wait_ge(sem("s_summed"), 2 * c + p + 1)
                        eng.wait_ge(sem("s_valued"), 2 * c + 1)
                        for o, (b, at, w) in enumerate(z_ops):
                            last = act(wt[p][:, at:at + w], bank[3 * p + b][:, 0:w], ACT.Exp)
                        last.then_inc(sem("s_exped"), 1)
                    eng.wait_ge(sem("s_valued"), 2 * c + 3)
                    act(col(a_hi, c), bank[6][:, :], ACT.Copy).then_inc(sem("s_out_hi"), 1)
                own.loop(0, 8, 6, body)

            def forgetting():
                def body(c):
                    exps(fprob[0], 8 * c, 0, "f_", 0)
                    exps(fprob[1], 8 * c, 1, "f_", 1)
                    for n in range(2):
                        copies(fprob_t, 8 * c, 2 * c, n, "f_")
                    eng.wait_ge(sem("f_valued"), 2 * c + 3)
                    act(col(a_hi, c), bank[7][:, :], ACT.Copy).then_inc(sem("f_out_hi"), 1)
                loop(eng, 0, 8, body)

            def ple(n):
                name = f"ple{n}"
                eng.wait_ge(sem("p_in"), 16 * n + 16)
                act(p_hi[:, :, :], p_raw[:, :, :], ACT.Copy).then_inc(sem("p_hi_done"), 1)
                norm(name, a_hi)
                for k in range(2):
                    ahead(name + "_proj", 0, k, 4)
                gate_tiles(name + "_gate", "x_done", x0[name + "_gate"])

            eng.dma_start(x[:, :, :], x_t).then_inc(sem("x_in"), 16)
            eng.dma_start(vec[:, :], vec_d).then_inc(sem("vec_in"), 16)
            eng.dma_start(con[:, :], con_d).then_inc(sem("const_in"), 16)
            eng.wait_ge(sem("const_in"), 16)
            act(mask_r[:, :], cst("below"), ACT.Copy).then_inc(sem("masks"), 1)
            act(ident_r[:, :], ident, ACT.Copy).then_inc(sem("masks"), 1)
            eng.wait_ge(sem("eps_set"), 1)
            split(0, 0, 4)
            split(1, 0, 4)
            eng.wait_ge(sem("table_stored"), 16)
            ffn(0)
            norm("mix", a_hi)
            project("qkv0")
            eng.wait_ge(sem("wg_in"), 16)
            act(wg_hi[:, :], wg_raw[:, :], ACT.Copy).then_inc(sem("wg_hi_done"), 1)
            eng.wait_ge(sem("gates_raw"), 1)
            act(gates[:, :, :], bank[7][:, 0:NTT * 48].rearrange("p (t n) -> p t n", n=48), ACT.Sigmoid)\
                .then_inc(sem("gates_ready"), 1)
            for kv in range(2):
                eng.wait_ge(sem("cw1_used"), 2 * kv + 2)
                for ht in range(2):
                    act(chid[:, ht, :, :], bank[4 + ht][:, 0:4 * NCMP].rearrange("p (g n) -> p g n", n=NCMP), ACT.Silu)\
                        .then_inc(sem("chid_ready"), 1)
                if kv == 0:
                    eng.wait_ge(sem("kcmp_raw"), 1)
                    act(csq[:, 0, :], bank[6][:, 0:2 * NCMP], ACT.Square).then_inc(sem("ksq_ready"), 1)
                    eng.wait_ge(sem("kcmp_mean"), 1)
                    own(act(csq[:, 1, :], bank[7][:, 0:2 * NCMP], ACT.Ln, bias=epsc[:, 0:1]))
                    act(csq[:, 1, :], csq[:, 1, :], ACT.Exp, scale=-0.5).then_inc(sem("kcmp_root"), 1)
                else:
                    eng.wait_ge(sem("vcmp_raw"), 1)
                    act(vcmp[0:NCMP, :], bank[6][0:NCMP, 0:256], ACT.Copy).then_inc(sem("vcmp_done"), 1)
            nsa()
            norm("mem", m_hi, NMEM)
            project("memkv", NMEM)
            project("qmem")
            mem_attention()
            gate_tiles("gnsa", "tile_taken", taken0["gnsa"])
            conv()
            eng.wait_ge(sem("tile_taken"), taken0["gmem"])
            gate_tiles("gmem", "tmp_ready", split_base["gmem"], b_hi)
            groups(eng, "wo0", 4, lambda i: [ahead("wo0", i, k, 4) for k in range(4)], 2)
            ffn(1)
            norm("attn0", a_hi)
            project("sb_qkv")
            stick_breaking()
            groups(eng, "sb_o", 4, lambda i: [ahead("sb_o", i, k, 4) for k in range(4)], 2)
            ffn(2)
            ple(0)
            norm("shared", a_hi)
            project("fox_kv")
            eng.wait_ge(sem("wf_in"), 16)
            act(wf_hi[:, :], wf_raw[:, :], ACT.Copy).then_inc(sem("wf_hi_done"), 1)
            eng.wait_ge(sem("f_biasadded"), 1)
            own(act(fl[:, 1, :], fl[:, 0, :], ACT.Abs))
            own(act(fl[:, 1, :], fl[:, 1, :], ACT.Exp, scale=-1.0))
            act(fl[:, 2, :], fl[:, 1, :], ACT.Ln, bias=1.0).then_inc(sem("f_softplus"), 1)
            norm("attn1", a_hi, mean=False)
            project("fox_q")
            forgetting()
            groups(eng, "fox_o", 4, lambda i: [ahead("fox_o", i, k, 4) for k in range(4)], 2)
            ffn(3)
            ple(1)

        @block.vector
        def _(eng):
            own = Link(eng, "vector_step")

            def wait(name, n):
                eng.wait_ge(sem(name), n)

            def square(c, first=False):
                if first:
                    own(eng.tensor_tensor(sqsum[:, :], x[:, c, :], x[:, c, :], ALU.mult))
                else:
                    own(eng.tensor_tensor(sqtmp[:, :], col(x, c), col(x, c), ALU.mult))
                    own(eng.tensor_tensor(sqsum[:, :], sqsum[:, :], sqtmp[:, :], ALU.add))

            def normalize(name, src, gain, hi, lo, n, used, mean=True):
                q = split_base[f"{name}_norm"]
                if mean:
                    wait("rstd_ready", mean_no[name] + 1)
                if used:
                    wait("unit_done", used)

                def rest(k):
                    wait("hi_done", q + k + 1)
                    eng.tensor_tensor(lo[:, k, :], tmp[k % 2][:, 0:n], hi[:, k, :].bitcast(F32), ALU.subtract)\
                        .then_inc(sem("lo_done"), 1)
                for k in range(NCH):
                    wait("lo_done", q + k + 1)
                    eng.scalar_tensor_tensor(out=tmp[k % 2][:, 0:n], in0=src[:, k, :], scalar=vcol(gain, k),
                                             in1=rstd[:, 0:n], op0=ALU.mult, op1=ALU.mult)\
                        .then_inc(sem("tmp_ready"), 1)
                    if k:
                        rest(k - 1)
                rest(NCH - 1)

            def update(name, factor, per=4):
                u, xb = U0[name], x0[name]
                two = UNITS[name] // NCH

                own(eng.memset(sqsum[:, :], 0.0))

                def body(i):
                    for k in range(4):
                        wait("unit_done", u + 4 * two * i + two * (k + 1))
                        eng.scalar_tensor_tensor(out=col(x, 4 * i + k), in0=bank[k][:, :], scalar=factor,
                                                 in1=col(x, 4 * i + k), op0=ALU.mult, op1=ALU.add)\
                            .then_inc(sem("x_done"), 1)
                        wait("x_done", xb + 4 * i + k + 1)
                        square(4 * i + k)
                own.loop(0, 2, 8, body)
                eng.sem_inc(sem("sqsum_done"), 1)

            def ffn(f, used):
                normalize(f"ffn{f}", x, f"ffn{f}", a_hi, a_lo, S, used)
                u, q = U0[f"ffn{f}_in"], split_base[f"ffn{f}"]

                def body(i):
                    for j in range(2):
                        h = 2 * i + j
                        wait("silu_done", NF * f + h + 1)
                        wait("unit_done", u + 4 * i + 2 * j + 2)
                        wait("lo_done", q + h + 1)
                        eng.tensor_tensor(tmp[j][:, :], act_t[j][:, :], bank[2 * j + 1][:, :], ALU.mult)\
                            .then_inc(sem("tmp_ready"), 1)
                        wait("hi_done", q + h + 1)
                        eng.tensor_tensor(col(h_lo, h), tmp[j][:, :], col(h_hi, h).bitcast(F32), ALU.subtract)\
                            .then_inc(sem("lo_done"), 1)
                loop(eng, 0, NF // 2, body)
                update(f"ffn{f}_out", 0.5 if f < 2 else 1.0)

            def project(name, n=S):
                u, ts, g, vn = U0[name], tiles[name], norm0[name], v0[name]
                group = []

                def taken(ins):
                    ins.then_inc(sem("tile_taken"), 1)

                for t, tile in enumerate(ts):
                    b = bank[t % 4]
                    if tile[0] == "norm":
                        group.append(t)
                        if len(group) < tile[4]:
                            continue
                        g += 1
                        wait("root_done", g)
                        for m in group:
                            taken(eng.scalar_tensor_tensor(out=ts[m][1], in0=bank[m % 4][:, 0:n], scalar=ts[m][2],
                                                           in1=tmp[(g - 1) % 2][:, 0:n], op0=ALU.mult, op1=ALU.mult))
                        group = []
                        continue
                    wait("unit_done", u + t + 1)
                    if tile[0] == "plain":
                        taken(eng.tensor_scalar(tile[1], b[:, :], tile[2], None, ALU.mult))
                    elif tile[0] == "v":
                        if vn >= 2:
                            wait("v_turned", vn - 1)
                        taken(eng.tensor_copy(vt[vn % 2][:, 0:n], b[:, 0:n]))
                        vn += 1
                    else:
                        _, dst, kv, pair = tile
                        for par in range(2):
                            r = slice(64 * par, 64 * par + 64)
                            eng.tensor_copy(dst[0:64, kv, 2 * pair + par, :], b[r, :])
                            last = eng.tensor_copy(dst[64:P, kv, 2 * pair + par, 0:S - 1], b[r, 1:S])
                        taken(last)
                        wait("tile_taken", taken0[name] + t + 1)

            def small_rest(lo, full, hi, ready, done):
                wait(ready, 1)
                eng.tensor_tensor(lo[:, :], full[:, :], hi[:, :].bitcast(F32), ALU.subtract).then_inc(sem(done), 1)

            def bias(pb, terms, i4, n, pre, slot):
                for i in range(4):
                    wait(pre + "scored", i4 + 4 * n + i + 2)
                    eng.sem_inc(sem(pre + "scores_seen"), 1)
                    w = (i + 1) * P
                    eng.tensor_tensor_reduce(pb[:, p_at[i]:p_at[i] + w], bank[i][:, 0:w], terms[:, (3 - i) * P:S],
                                             1.0, HUGE, ALU.add, ALU.min, stat[:, 4 * slot + i:4 * slot + i + 1])\
                        .then_inc(sem(pre + "biased"), 1)

            def scale(pb, i4, n, pre, slot, gate=None):
                s4 = slice(8 + 4 * slot, 12 + 4 * slot)
                wait(pre + "exped", i4 + 4 * n + 4)
                own(eng.reciprocal(stat[:, s4], stat[:, s4]))
                if gate is not None:
                    own(eng.tensor_tensor(stat[:, s4], stat[:, s4], gate, ALU.mult))
                for i in range(4):
                    v = pb[:, p_at[i]:p_at[i] + (i + 1) * P]
                    eng.tensor_scalar(v, v, stat[:, 8 + 4 * slot + i:9 + 4 * slot + i], None, ALU.mult)\
                        .then_inc(sem(pre + "scaled"), 1)

            def nsa():
                wait("vcmp_done", 1)
                for a in range(2):
                    def body(r, a=a):
                        c = 4 * a + r

                        def gate(par, branch):
                            return gates[:, :, bass.ds((8 * a + 4 * par + r) * 3 + branch, 1)].rearrange("p t a -> p (t a)")

                        def cmp_bias(par):
                            cs, mn = cprob[:, par], stat[:, 32 + 4 * par:36 + 4 * par]
                            wait("n_strips", 32 * c + 32)
                            wait("n_cscored", 2 * c + par + 1)
                            for i in range(NTT):
                                at = 415 - P * i
                                last = eng.tensor_tensor(cs[:, i, :], bank[6][:, i * 32:i * 32 + NCMP],
                                                         strip[:, par, at:at + 16 * NCMP - 15:16], ALU.add)
                            last.then_inc(sem("n_cadded"), 1)
                            wait("n_cadded", 2 * c + par + 2)
                            own(eng.tensor_reduce(mn, cs, AX.X, ALU.min))
                            for i in range(NTT):
                                last = eng.tensor_scalar(cs[:, i, :], cs[:, i, :], stat[:, 32 + 4 * par + i:33 + 4 * par + i],
                                                         None, ALU.subtract)
                            last.then_inc(sem("n_cmin"), 1)

                        def cmp_scale(par):
                            cs, sm = cprob[:, par], stat[:, 48 + 4 * par:52 + 4 * par]
                            wait("n_cexped", 2 * c + par + 1)
                            own(eng.tensor_reduce(sm, cs, AX.X, ALU.add))
                            own(eng.reciprocal(sm, sm))
                            own(eng.tensor_tensor(sm, sm, gate(par, 0), ALU.mult))
                            own(eng.tensor_tensor(sm, sm, vcol("anyv", 0, 4), ALU.mult))
                            for i in range(NTT):
                                last = eng.tensor_scalar(cs[:, i, :], cs[:, i, :], stat[:, 48 + 4 * par + i:49 + 4 * par + i],
                                                         None, ALU.mult)
                            last.then_inc(sem("n_cscaled"), 1)

                        def biased(n):
                            if n >= 2:
                                wait("n_turned", 16 * c + 4 * n - 4)
                            bias(prob[n % 2], strip[:, n // 2, :], 16 * c, n, "n_", n % 2)

                        def scaled(n):
                            scale(prob[n % 2], 16 * c, n, "n_", n % 2, gate(n // 2, 1 + n % 2))

                        cmp_bias(0)
                        biased(0)
                        biased(1)
                        cmp_bias(1)
                        cmp_scale(0)
                        scaled(0)
                        biased(2)
                        scaled(1)
                        biased(3)
                        cmp_scale(1)
                        scaled(2)
                        scaled(3)
                        wait("n_valued", 4 * c + 5)
                        eng.tensor_copy(col(mixed, c), bank[7][:, :]).then_inc(sem("n_out_taken"), 1)
                    own.loop(0, 4, 2 * 1 + 2 * 4 + 4 * 2, body)

            def mem_attention():
                def low(t):
                    wait("m_scored", t + 1)
                    eng.tensor_reduce(stat[:, t:t + 1], bank[4 + t % 2][:, 0:NMEM], AX.X, ALU.min)\
                        .then_inc(sem("m_min"), 1)

                def high(t):
                    wait("m_exped", t + 1)
                    own(eng.reciprocal(stat[:, 16 + t:17 + t], stat[:, 16 + t:17 + t]))
                    eng.tensor_scalar(mprob[t % 2][:, :], mprob[t % 2][:, :], stat[:, 16 + t:17 + t], None, ALU.mult)\
                        .then_inc(sem("m_scaled"), 1)

                def out(a):
                    wait("m_valued", 2 * a + 2)
                    for r in range(4):
                        eng.tensor_copy(om[:, 4 * a + r, :], bank[r][:, :]).then_inc(sem("m_out_taken"), 1)
                for t in range(4 * MH):
                    low(t)
                    if t:
                        high(t - 1)
                    if t == 10:
                        out(0)
                high(4 * MH - 1)
                out(1)

            def gnsa():
                tk = taken0["gnsa"]

                def body(i):
                    for k in range(4):
                        wait("sigmoid_done", gates0["gnsa"] + 4 * i + k + 1)
                        eng.tensor_tensor(col(mixed, 4 * i + k), col(mixed, 4 * i + k), act_t[k % 2][:, :], ALU.mult)\
                            .then_inc(sem("tile_taken"), 1)
                loop(eng, 0, 2, body)
                wait("tile_taken", tk + 8)

            def conv():
                u, tk = U0["conv"], taken0["conv"]
                own(eng.memset(cu[:, 0:2], 0.0))

                def body(i):
                    def w(k):
                        return vec[:, bass.ds(VEC["convw"] + 8 * k + i, 1)]
                    wait("gates_copied", 2 * i + 2)
                    wait("unit_done", u + 4 * i + 3)
                    eng.tensor_tensor(cu[:, 2:S + 2], act_t[0][:, :], bank[2][:, :], ALU.mult).then_inc(sem("tile_taken"), 3)
                    wait("tile_taken", tk + 4 * i + 3)
                    own(eng.tensor_scalar(cy[:, :], cu[:, 2:S + 2], w(2), vec[:, bass.ds(VEC["convb"] + i, 1)],
                                          ALU.mult, ALU.add))
                    for k in (1, 0):
                        own(eng.scalar_tensor_tensor(out=cy[:, :], in0=cu[:, k:S + k], scalar=w(k), in1=cy[:, :],
                                                     op0=ALU.mult, op1=ALU.add))
                    own(eng.tensor_tensor(cy[:, :], cy[:, :], cb[:, :], ALU.mult))
                    wait("sigmoid_conv", i + 1)
                    eng.tensor_tensor(cy[:, :], cy[:, :], act_t[1][:, :], ALU.mult).then_inc(sem("tile_taken"), 1)
                    wait("tile_taken", tk + 4 * i + 4)
                    own(eng.tensor_tensor(col(mixed, i), col(mixed, i), cy[:, :], ALU.add))
                own.loop(0, 8, 5, body)

            def gmem():
                q, tk = split_base["gmem"], taken0["gmem"]

                def body(i):
                    for k in range(4):
                        c = 4 * i + k
                        wait("sigmoid_done", gates0["gmem"] + c + 1)
                        eng.tensor_tensor(act_t[k % 2][:, :], act_t[k % 2][:, :], col(om, c), ALU.mult)\
                            .then_inc(sem("tile_taken"), 1)
                        wait("tile_taken", tk + c + 1)
                        wait("lo_done", q + c + 1)
                        eng.tensor_tensor(tmp[k % 2][:, :], col(mixed, c), act_t[k % 2][:, :], ALU.add)\
                            .then_inc(sem("tmp_ready"), 1)
                        wait("hi_done", q + c + 1)
                        eng.tensor_tensor(col(b_lo, c), tmp[k % 2][:, :], col(b_hi, c).bitcast(F32), ALU.subtract)\
                            .then_inc(sem("lo_done"), 1)
                loop(eng, 0, 2, body)

            def stick_breaking():
                def body(c):
                    for p in range(2):
                        wait("s_z", 2 * c + p + 2)
                        for b, at, w in z_ops:
                            eng.tensor_scalar(sp[p][:, at:at + w], bank[3 * p + b][:, 0:w], 40.0, None, ALU.min)\
                                .then_inc(sem("s_min"), 1)
                    for p in range(2):
                        for o, (b, at, w) in enumerate(z_ops):
                            wait("s_log", 6 * c + 3 * p + o + 1)
                            last = eng.tensor_tensor(sp[p][:, at:at + w], bank[3 * p + b][:, 0:w], sp[p][:, at:at + w], ALU.max)
                        last.then_inc(sem("s_soft"), 1)
                    wait("s_out_hi", c + 1)
                    eng.tensor_tensor(col(a_lo, c), bank[6][:, :], col(a_hi, c).bitcast(F32), ALU.subtract)\
                        .then_inc(sem("s_out_taken"), 1)
                loop(eng, 0, 8, body)

            def forgetting():
                def body(c):
                    for n in range(2):
                        bias(fprob[n], cst("causal", S), 8 * c, n, "f_", n)
                    for n in range(2):
                        scale(fprob[n], 8 * c, n, "f_", n)
                    wait("f_out_hi", c + 1)
                    eng.tensor_tensor(col(a_lo, c), bank[7][:, :], col(a_hi, c).bitcast(F32), ALU.subtract)\
                        .then_inc(sem("f_out_taken"), 1)
                own.loop(0, 8, 2, body)

            def ple(n, used):
                name = f"ple{n}"
                wait("p_hi_done", n + 1)
                eng.tensor_tensor(p_lo[:, :, :], p_raw[:, :, :], p_hi[:, :, :].bitcast(F32), ALU.subtract)\
                    .then_inc(sem("p_split"), 1)
                normalize(name, x, name, a_hi, a_lo, S, used)
                u, xb = U0[name + "_proj"], x0[name + "_gate"]
                for t in range(8):
                    wait("unit_done", u + t // 4 + 1)
                    eng.tensor_copy(proj[:, t, :], bank[t % 4][:, :]).then_inc(sem("tile_taken"), 1)
                wait("tile_taken", taken0[name + "_proj"] + 8)
                own(eng.memset(sqsum[:, :], 0.0))

                def body(i):
                    for k in range(4):
                        c = 4 * i + k
                        wait("sigmoid_done", gates0[name + "_gate"] + c + 1)
                        own(eng.tensor_tensor(act_t[k % 2][:, :], act_t[k % 2][:, :], col(proj, c), ALU.mult))
                        eng.tensor_tensor(col(x, c), col(x, c), act_t[k % 2][:, :], ALU.add).then_inc(sem("x_done"), 1)
                        wait("x_done", xb + c + 1)
                        square(c)
                own.loop(0, 2, 12, body)
                eng.sem_inc(sem("sqsum_done"), 1)

            for name, n in (("x_done", 4), ("tile_taken", 4), ("lo_done", 2), ("n_biased", 4), ("f_biased", 4),
                            ("n_copied", 2), ("f_copied", 2), ("n_cadded", 1), ("n_out_taken", 1), ("s_exped", 2),
                            ("s_out_taken", 1), ("f_out_taken", 1)):
                eng.sem_inc(sem(name), n)
            eng.memset(epsc[:, :], EPS).then_inc(sem("eps_set"), 1)
            wait("table_raw", 1)
            for h in range(2):
                eng.tensor_copy(table[:, h * 512:(h + 1) * 512], bank[6 + h][0:NH, :]).then_inc(sem("table_ready"), 1)
            wait("vec_in", 16)
            own(eng.tensor_scalar(negq[:, :], vcol("qn"), -HD ** -0.5, None, ALU.mult))
            own(eng.tensor_scalar(negfq[:, :], vcol("fq"), -HD ** -0.5, None, ALU.mult))
            own(eng.tensor_scalar(negmq[:, :], vcol("mq", 0, 2), -256 ** -0.5, None, ALU.mult))
            wait("x_in", 16)
            for c in range(NCH):
                square(c, c == 0)
            eng.sem_inc(sem("sqsum_done"), 1)
            ffn(0, 0)
            normalize("mix", x, "mix", a_hi, a_lo, S, U0["qkv0"])
            project("qkv0")
            small_rest(wg_lo, wg_raw, wg_hi, "wg_hi_done", "wg_split")
            for kv in range(2):
                if kv:
                    wait("cw1_used", 2)
                last = None
                for j in range(16):
                    last = eng.tensor_scalar(xc[:, j], cc[:, kv, :, 2 * j:2 * j + 16 * NCMP - 15:16],
                                             vcol("pek" if kv == 0 else "pev", j), None, ALU.add)
                last.then_inc(sem("xc_ready"), 1)
                if kv == 0:
                    wait("kcmp_root", 1)
                    eng.scalar_tensor_tensor(out=kcmp[:, :, 0:NCMP],
                                             in0=bank[6][:, 0:2 * NCMP].rearrange("p (c n) -> p c n", n=NCMP),
                                             scalar=vcol("kn"), in1=csq[:, 1, :].rearrange("p (c n) -> p c n", n=NCMP),
                                             op0=ALU.mult, op1=ALU.mult).then_inc(sem("kcmp_done"), 1)
            nsa()
            wait("mem_in", 16)
            own(eng.memset(sqsum[:, :], 0.0))
            for c in range(NCH):
                own(eng.tensor_tensor(sqtmp[:, 0:NMEM], memx[:, c, :], memx[:, c, :], ALU.mult))
                own(eng.tensor_tensor(sqsum[:, 0:NMEM], sqsum[:, 0:NMEM], sqtmp[:, 0:NMEM], ALU.add))
            eng.sem_inc(sem("sqsum_done"), 1)
            normalize("mem", memx, "mem", m_hi, m_lo, NMEM, 0)
            project("memkv", NMEM)
            project("qmem")
            mem_attention()
            gnsa()
            conv()
            gmem()
            update("wo0", 1.0)
            ffn(1, U0["wo0"])
            normalize("attn0", x, "attn0", a_hi, a_lo, S, U0["sb_qkv"])
            project("sb_qkv")
            stick_breaking()
            update("sb_o", 1.0)
            ffn(2, U0["ffn2_in"])
            ple(0, U0["ple0_proj"])
            normalize("shared", x, "shared", a_hi, a_lo, S, U0["fox_kv"])
            project("fox_kv")
            small_rest(wf_lo, wf_raw, wf_hi, "wf_hi_done", "wf_split")
            wait("f_raw", 1)
            eng.tensor_tensor(fl[:, 0, :], bank[7][:, 0:NTT * NH], vcol("bf", 0, 64), ALU.add).then_inc(sem("f_biasadded"), 1)
            wait("f_softplus", 1)
            eng.scalar_tensor_tensor(out=fl[:, 1, :], in0=fl[:, 0, :], scalar=0.0, in1=fl[:, 2, :], op0=ALU.min,
                                     op1=ALU.subtract).then_inc(sem("log_f"), 1)
            normalize("attn1", x, "attn1", a_hi, a_lo, S, U0["fox_q"], mean=False)
            wait("fcum_raw", 1)
            eng.tensor_copy(fcum[:, :], bank[7][0:NH, :]).then_inc(sem("fcum_ready"), 1)
            project("fox_q")
            forgetting()
            update("fox_o", 1.0)
            ffn(3, U0["ffn3_in"])
            ple(1, U0["ple1_proj"])

        @block.gpsimd
        def _(eng):
            def rest(v, i):
                nk = BLOCKS[v]
                eng.wait_ge(sem("w_hi_ready"), v + 4 * i + 1)
                eng.tensor_tensor(w_lo[v % 2][:, 0:nk * P], raw[v % 4][:, 0:nk * P],
                                  w_hi[v % 2][:, 0:nk * P].bitcast(F32), ALU.subtract).then_inc(sem("w_lo_ready"), 1)

            def rests(a, b):
                b = min(b, NU)
                while a < b:
                    n = 1
                    while a + n < b and BLOCKS[a + n] == BLOCKS[a]:
                        n += 1

                    def body(i, a=a):
                        for k in range(4):
                            rest(a + k, i)
                    loop(eng, 0, n // 4, body)
                    for v in range(a + n // 4 * 4, a + n):
                        rest(v, 0)
                    a += n

            eng.dma_start(rel[:, :], rel_d).then_inc(sem("rel_in"), 16)
            eng.dma_start(hot[:, :], hot_d).then_inc(sem("rel_in"), 16)
            eng.wait_ge(sem("table_ready"), 2)
            eng.dma_start(table_d[:, :], table[:, :]).then_inc(sem("table_stored"), 16)
            rests(0, 2)
            eng.wait_ge(sem("table_stored"), 16)
            for h in range(0, NH, 4):
                src = bass.AP(tensor=table_d, offset=h * 1024, ap=[[1024, 4], [0, P], [1, 1024]])
                dst = rows_d[h:h + 4, :].rearrange("h (p n) -> h p n", n=1024)
                eng.dma_start(dst, src).then_inc(sem("rows_stored"), 16)
            rests(2, U0["qkv0"] + 2)
            eng.wait_ge(sem("unit_done"), U0["qkv0"])
            eng.dma_start(wg_raw[:, :], wg_d).then_inc(sem("wg_in"), 16)
            eng.dma_start(cw2[:, :, :, :], cw2_d).then_inc(sem("cw2_in"), 16)
            for half in range(2):
                eng.dma_start(cw1[half][:, :, :], cw1_d[half]).then_inc(sem(f"cw1_in{half}"), 16)
            rests(U0["qkv0"] + 2, U0["memkv"] + 2)
            for half in range(2):
                eng.wait_ge(sem("cw1_used"), half + 1)
                eng.dma_start(cw1[half][:, :, :], cw1_d[2 + half]).then_inc(sem(f"cw1_in{half}"), 16)
            eng.wait_ge(sem("rows_stored"), 16 * 4)
            eng.wait_ge(sem("vcmp_done"), 1)
            for a in range(2):
                def body(r, a=a):
                    c = 4 * a + r
                    eng.wait_ge(sem("n_scored"), 16 * c + 1)
                    eng.wait_ge(sem("n_biased"), 16 * c + 4)
                    eng.tensor_copy(q_st[:, :], col(q_t, c)).then_inc(sem("q_staged"), 1)
                    for par in range(2):
                        h = 8 * a + 4 * par + r
                        src = rows_d[bass.ds(h, 1), 127:127 + P * 1023].rearrange("a (p n) -> p (a n)", n=1023)
                        eng.dma_start(strip[:, par, :], src[:, 0:STRIP]).then_inc(sem("n_strips"), 16)
                loop(eng, 0, 4, body)
            eng.wait_ge(sem("n_out_taken"), 9)
            eng.dma_start(memx[:, :, :], mem_t).then_inc(sem("mem_in"), 16)
            rests(U0["memkv"] + 2, U0["sb_o"] + 2)

            def stage(pre, extra=None):
                def body(c):
                    eng.wait_ge(sem(pre + ("z" if pre == "s_" else "scored")), (2 if pre == "s_" else 8) * c + 1)
                    eng.wait_ge(sem(pre + "valued"), 2 * c + 1)
                    if extra:
                        extra(c)
                    eng.tensor_copy(ks2[:, :], col(k2, c))
                    eng.tensor_copy(qs2[:, :], col(q2, c))
                    eng.tensor_copy(vs2[:, :, :], v2[:, :, bass.ds(c * P, P)]).then_inc(sem(pre + "staged"), 1)
                loop(eng, 0, 8, body)

            eng.wait_ge(sem("tile_taken"), taken0["sb_qkv"] + 24)
            eng.wait_ge(sem("vtok_done"), v0["fox_kv"])
            stage("s_")
            rests(U0["sb_o"] + 2, U0["ple0_proj"] + 2)
            eng.wait_ge(sem("unit_done"), U0["ple0_proj"])
            eng.dma_start(p_raw[:, :, :], p_t[0]).then_inc(sem("p_in"), 16)
            rests(U0["ple0_proj"] + 2, U0["fox_kv"] + 2)
            eng.wait_ge(sem("x_done"), x0["ple0_gate"] + 8)
            eng.dma_start(wf_raw[:, :], wf_d).then_inc(sem("wf_in"), 16)
            eng.dma_start(augq[1:2, :, :], aug_d[0:1]).then_inc(sem("f_aug"), 16)
            eng.dma_start(augk[0:1, :, :], aug_d[1:2]).then_inc(sem("f_aug"), 16)
            rests(U0["fox_kv"] + 2, U0["fox_q"] + 2)
            eng.wait_ge(sem("fcum_ready"), 1)
            eng.dma_start(fcum_d[:, :], fcum[:, :]).then_inc(sem("fcum_stored"), 16)
            rests(U0["fox_q"] + 2, U0["fox_o"] + 2)
            eng.wait_ge(sem("fcum_stored"), 16)

            def forget_rows(c):
                src = fcum_d[bass.ds(2 * c, 2), :].rearrange("(a h) n -> a h n", a=1)
                eng.dma_start(augq[0:1, :, :], src).then_inc(sem("f_aug"), 16)
                eng.dma_start(augk[1:2, :, :], src).then_inc(sem("f_aug"), 16)
            eng.wait_ge(sem("tile_taken"), taken0["fox_q"] + 8)
            eng.wait_ge(sem("vtok_done"), v0["fox_q"])
            stage("f_", forget_rows)
            rests(U0["fox_o"] + 2, U0["ple1_proj"] + 2)
            eng.wait_ge(sem("unit_done"), U0["ple1_proj"])
            eng.dma_start(p_raw[:, :, :], p_t[1]).then_inc(sem("p_in"), 16)
            rests(U0["ple1_proj"] + 2, NU)


def constants():
    con = np.zeros((P, NCON), np.float32)
    r, c = np.arange(P)[:, None], np.arange(P)[None, :]

    def put(name, v):
        con[:, CON[name]:CON[name] + v.shape[1]] = v
    put("ident", np.eye(P))
    put("mean_d", np.full((P, P), 1.0 / D))
    put("mean_head", (r // HD == c // HD) / HD)
    put("mean_mem", np.full((P, P), 1.0 / 256))
    put("neg_tri", -1.0 * (r >= c))
    put("neg_ones", np.full((P, P), -1.0))
    put("below", -BIG * (c >= r))
    c4 = np.arange(S)[None, :]
    put("cum", 1.0 * (c4 >= r))
    put("causal", BIG * (384 + r - c4 < 0))
    dist = 511 - np.arange(1024)
    n = np.maximum(dist, 0)
    large = 16 + (np.log(np.maximum(n, 1).astype(np.float32) / 16) / np.float32(np.log(128 / 16))
                  * 16).astype(np.int32)
    bucket = np.where(n < 16, n, np.minimum(large, NREL - 1))
    hot = np.zeros((33, 1024), np.float32)
    hot[np.where(dist >= 0, bucket, 32), np.arange(1024)] = -1.0
    aug = np.ones((2, 2, S), np.float32)
    aug[1] = -1.0
    return con, hot, aug


def kernel(**inputs):
    import concourse.bacc as _bacc
    from concourse.bass_utils import run_bass_kernel_spmd as _run

    a = {k: np.asarray(v) for k, v in inputs.items()}

    def blocks(w, cols=None):
        k, m = w.shape
        return w.reshape(k // P, P, m // P, P).transpose(2, 1, 0, 3).reshape(m // P, P, k)

    def ffn_in(w):
        b = blocks(w)
        return np.stack([b[:NF], b[NF:]], 1).reshape(2 * NF, P, D)

    def ffn_out(w):
        b = blocks(w).reshape(NCH, P, 2, K11 * P)
        return b.transpose(0, 2, 1, 3).reshape(2 * NCH, P, K11 * P)

    def proj(w):
        return w.reshape(2, P, 2, 4, P).transpose(2, 1, 3, 0, 4).reshape(2, P, D)

    perm = np.concatenate([np.arange(HD) + HD * h for x in range(2) for r in range(4)
                           for h in (8 * x + r, 8 * x + 4 + r)])
    w_in = a["w_in"][0]
    at = np.cumsum([0, 1024, 1536, 48, 3072, 1024, 3072])
    wq, wkv, wg, wc, wqm, wm = (w_in[:, at[i]:at[i + 1]] for i in range(6))
    conv = np.stack([blocks(wc[:, :D][:, perm]), blocks(wc[:, D:2 * D][:, perm]), blocks(wc[:, 2 * D:][:, perm]),
                     blocks(wm[:, D:2 * D][:, perm])], 1).reshape(32, P, D)
    kvf = a["shared_w_kvf_2"]
    w8 = np.concatenate([
        ffn_in(a["ffn1_w_in"][0]), blocks(wq[:, perm]), blocks(wkv), blocks(a["w_mem_kv"][0]), blocks(wqm),
        blocks(wm[:, :D][:, perm]), conv, blocks(wm[:, 2 * D:][:, perm]), blocks(a["w_out"][0][perm]),
        ffn_in(a["ffn2_w_in"][0]),
        blocks(a["sb_w_qkv_2"][0]), blocks(a["sb_w_o_2"][0]), ffn_in(a["ffn_w_gu_2"][0]),
        proj(a["ple_w_proj_2"][0]), blocks(a["ple_w_gate_2"][0]),
        blocks(kvf[:, :2 * D]), blocks(a["fox_w_q_2"][0]), blocks(a["fox_w_o_2"][0]), ffn_in(a["ffn_w_gu_2"][1]),
        proj(a["ple_w_proj_2"][1]), blocks(a["ple_w_gate_2"][1])])
    w11 = np.concatenate([ffn_out(a["ffn1_w_out"][0]), ffn_out(a["ffn2_w_out"][0]), ffn_out(a["ffn_w_d_2"][0]),
                          ffn_out(a["ffn_w_d_2"][1])])

    def cols(v):
        return v.reshape(-1, P).T

    def twice(v):
        return np.concatenate([v, v])[:, None]

    def pe(v):
        return np.pad(v.reshape(16, P).T, ((0, 0), (0, 16)))

    anyv = np.ones((P, 4), np.float32)
    anyv[:31, 0] = 0.0
    vec = np.concatenate([
        cols(a["ffn1_norm_g"][0]), cols(a["mix_norm_g"][0]), cols(a["ffn2_norm_g"][0]), cols(a["attn_norm_g_2"][0]),
        cols(a["attn_norm_g_2"][1]), cols(a["shared_norm_g_2"]), cols(a["ffn_norm_g_2"][0]), cols(a["ffn_norm_g_2"][1]),
        cols(a["ple_norm_g_2"][0]), cols(a["ple_norm_g_2"][1]), cols(a["mem_norm_g"][0]),
        cols(a["conv_w"][0][:, perm]), cols(a["conv_b"][0][perm]),
        twice(a["q_norm_g"][0]), twice(a["k_norm_g"][0]), cols(a["mem_q_norm_g"][0]), cols(a["mem_k_norm_g"][0]),
        twice(a["shared_k_norm_g_2"]), twice(a["fox_q_norm_g_2"][0]), pe(a["cmp_pe_k"][0]), pe(a["cmp_pe_v"][0]),
        np.tile(a["shared_b_f_2"], (P, 4)), anyv], 1)
    con, hot, aug = constants()

    def w1(w):
        return w.reshape(2, 8, P, 256).transpose(0, 2, 1, 3)

    arrays = {
        "w8": w8, "w11": w11,
        "x_t": a["x"][0].T.reshape(NCH, P, S).transpose(1, 0, 2),
        "mem_t": a["mem"][0].T.reshape(NCH, P, NMEM).transpose(1, 0, 2),
        "p_t": a["p_2"][:, 0].transpose(0, 2, 1).reshape(2, 2, P, S).transpose(0, 2, 1, 3),
        "vec": vec, "con": con,
        "wg": wg.reshape(NCH, P, 48).transpose(1, 0, 2).reshape(P, NCH * 48),
        "wf": kvf[:, 2 * D:].reshape(NCH, P, NH).transpose(1, 0, 2).reshape(P, NCH * NH),
        "cw1": np.concatenate([w1(a["cmp_w1_k"][0]), w1(a["cmp_w1_v"][0])]),
        "cw2": np.stack([w.reshape(2, P, HD).transpose(1, 0, 2) for w in (a["cmp_w2_k"][0], a["cmp_w2_v"][0])], 1),
        "rel": np.concatenate([a["rel_bias"], np.full((1, NH), -BIG, np.float32)]),
        "hot": hot, "aug": aug,
    }
    arrays = {k: np.ascontiguousarray(v) for k, v in arrays.items()}
    nc = _bacc.Bacc("TRN2", target_bir_lowering=False, num_devices=1)
    args = [nc.dram_tensor("in_" + k, v.shape, F32, kind="ExternalInput").ap() for k, v in arrays.items()]
    out = nc.dram_tensor("out_t", (P, NCH, S), F32, kind="ExternalOutput").ap()
    build(nc, *args, out)
    r = _run(nc, [{"in_" + k: v for k, v in arrays.items()}], core_ids=[0])
    got = np.asarray(r.results[0]["out_t"])
    return np.ascontiguousarray(got.transpose(2, 1, 0).reshape(1, S, D))
```
